# Optimizing a Trainium2 kernel written in Bass

```python
import jax, jax.numpy as jnp
from jax import lax
import numpy as np

D_MODEL = 1024
BATCH = 1
SEQ = 512
DEPTH = 2
DEC_BATCH = 1
DEC_SEQ = 64
PAST_LEN = 256

CHUNK = 64
N_A = DEPTH // 2
N_B = DEPTH - N_A
A_HEADS = 16
Q_LORA = 384
KV_LORA = 256
NOPE_DIM = 64
ROPE_DIM = 32
V_DIM = 64
QK_DIM = NOPE_DIM + ROPE_DIM
ROPE_THETA = 10000.0
Q_BLOCK = 128
B_HEADS = 16
B_HEAD_DIM = D_MODEL // B_HEADS
LEFT_CHUNKS = 8
B_WINDOW = LEFT_CHUNKS * CHUNK
REL_CLIP = 128
P_HEADS = 8
N_KEYS = 128
N_EXPERTS = N_KEYS * N_KEYS
P_DKEY = 128
P_HALF = P_DKEY // 2
P_TOPK = 16
PEER_BLOCK = 128
NEG = -1e30

kernel_name = "yoco_mla_band_peer_stream_step"

def rmsnorm(x, w, eps=1e-6):
    xf = x.astype(jnp.float32)
    y = xf * lax.rsqrt(jnp.mean(xf * xf, axis=-1, keepdims=True) + eps)
    return (y * w.astype(jnp.float32)).astype(x.dtype)

def modulate(x, w, shift, scale):
    return rmsnorm(x, w) * (1 + scale[:, None, :]) + shift[:, None, :]

def rope(x, pos):
    half = ROPE_DIM // 2
    freqs = ROPE_THETA ** (-jnp.arange(half, dtype=jnp.float32) / half)
    ang = pos.astype(jnp.float32)[:, None] * freqs[None, :]
    cos = jnp.cos(ang)[:, None, :].astype(x.dtype)
    sin = jnp.sin(ang)[:, None, :].astype(x.dtype)
    x1, x2 = x[..., :half], x[..., half:]
    return jnp.concatenate([x1 * cos - x2 * sin, x2 * cos + x1 * sin], axis=-1)

def mla_attention(q, k, v, q_pos, k_pos):
    B, T, H, E = q.shape
    qb = min(Q_BLOCK, T)
    nb = T // qb
    scale = E ** -0.5
    k_chunk = k_pos // CHUNK

    def one_block(args):
        qi, pi = args
        s = jnp.einsum('bqhe,bshe->bhqs', qi, k, preferred_element_type=jnp.float32) * scale
        allowed = k_chunk[None, :] <= (pi // CHUNK)[:, None]
        s = jnp.where(allowed[None, None], s, NEG)
        p = jax.nn.softmax(s, axis=-1).astype(v.dtype)
        return jnp.einsum('bhqs,bshd->bqhd', p, v)

    qs = q.reshape(B, nb, qb, H, E).transpose(1, 0, 2, 3, 4)
    ps = q_pos.reshape(nb, qb)
    out = lax.map(one_block, (qs, ps))
    return out.transpose(1, 0, 2, 3, 4).reshape(B, T, H, v.shape[-1])

def mla_mixer(h, pos, past_ckv, past_kr, w_in, q_lora_norm, kv_lora_norm, w_uq, w_ukv, q_norm, k_norm, w_o):
    B, T, _ = h.shape
    proj = h @ w_in
    c_q = rmsnorm(proj[..., :Q_LORA], q_lora_norm)
    c_kv = rmsnorm(proj[..., Q_LORA:Q_LORA + KV_LORA], kv_lora_norm)
    k_r = proj[..., Q_LORA + KV_LORA:]
    if past_ckv is None:
        ckv_all, kr_all, k_pos = c_kv, k_r, pos
    else:
        P = past_ckv.shape[1]
        ckv_all = jnp.concatenate([past_ckv, c_kv], axis=1)
        kr_all = jnp.concatenate([past_kr, k_r], axis=1)
        k_pos = jnp.concatenate([jnp.arange(P, dtype=jnp.int32), pos])
    S = ckv_all.shape[1]
    q = (c_q @ w_uq).reshape(B, T, A_HEADS, QK_DIM)
    kv = (ckv_all @ w_ukv).reshape(B, S, A_HEADS, NOPE_DIM + V_DIM)
    k_nope, v = kv[..., :NOPE_DIM], kv[..., NOPE_DIM:]
    k = jnp.concatenate([k_nope, jnp.broadcast_to(kr_all[:, :, None, :], (B, S, A_HEADS, ROPE_DIM))], axis=-1)
    q = rmsnorm(q, q_norm)
    k = rmsnorm(k, k_norm)
    q = jnp.concatenate([q[..., :NOPE_DIM], rope(q[..., NOPE_DIM:], pos)], axis=-1)
    k = jnp.concatenate([k[..., :NOPE_DIM], rope(k[..., NOPE_DIM:], k_pos)], axis=-1)
    o = mla_attention(q, k, v, pos, k_pos)
    return o.reshape(B, T, A_HEADS * V_DIM) @ w_o, c_kv, k_r

def band_attend(q, k, v, q_pos, k_pos, bias_table):
    scale = q.shape[-1] ** -0.5
    s = jnp.einsum('bthe,bshe->bhts', q, k, preferred_element_type=jnp.float32) * scale
    rel = jnp.clip(q_pos[:, None] - k_pos[None, :], -REL_CLIP, REL_CLIP) + REL_CLIP
    s = s + bias_table[:, rel].astype(jnp.float32)[None]
    qc = q_pos // CHUNK
    kc = k_pos // CHUNK
    allowed = (k_pos[None, :] >= 0) & (kc[None, :] <= qc[:, None]) & (kc[None, :] >= qc[:, None] - LEFT_CHUNKS)
    s = jnp.where(allowed[None, None], s, NEG)
    p = jax.nn.softmax(s, axis=-1).astype(v.dtype)
    return jnp.einsum('bhts,bshe->bthe', p, v)

def band_attention_prompt(q, k, v, bias_table):
    B, T, H, E = q.shape
    nc = T // CHUNK
    band = (LEFT_CHUNKS + 1) * CHUNK
    kp = jnp.pad(k, ((0, 0), (B_WINDOW, 0), (0, 0), (0, 0)))
    vp = jnp.pad(v, ((0, 0), (B_WINDOW, 0), (0, 0), (0, 0)))
    qs = q.reshape(B, nc, CHUNK, H, E).transpose(1, 0, 2, 3, 4)

    def one_chunk(args):
        n, qn = args
        kn = lax.dynamic_slice_in_dim(kp, n * CHUNK, band, axis=1)
        vn = lax.dynamic_slice_in_dim(vp, n * CHUNK, band, axis=1)
        q_pos = n * CHUNK + jnp.arange(CHUNK, dtype=jnp.int32)
        k_pos = n * CHUNK - B_WINDOW + jnp.arange(band, dtype=jnp.int32)
        return band_attend(qn, kn, vn, q_pos, k_pos, bias_table)

    out = lax.map(one_chunk, (jnp.arange(nc, dtype=jnp.int32), qs))
    return out.transpose(1, 0, 2, 3, 4).reshape(B, T, H, E)

def band_mixer(h, pos, k_all, v_all, k_pos, w_q, q_norm, rel_bias, w_o, prompt):
    B, T, _ = h.shape
    q = rmsnorm((h @ w_q).reshape(B, T, B_HEADS, B_HEAD_DIM), q_norm)
    if prompt:
        o = band_attention_prompt(q, k_all, v_all, rel_bias)
    else:
        o = band_attend(q, k_all, v_all, pos, k_pos, rel_bias)
    return o.reshape(B, T, B_HEADS * B_HEAD_DIM) @ w_o

def shared_kv(x, c, kv_ada_w, kv_ada_b, kv_norm_w, w_kv, k_norm):
    B, T, _ = x.shape
    mod = jax.nn.silu(c) @ kv_ada_w + kv_ada_b
    shift, scale = jnp.split(mod, 2, axis=-1)
    h = modulate(x, kv_norm_w, shift, scale)
    kv = (h @ w_kv).reshape(B, T, 2, B_HEADS, B_HEAD_DIM)
    return rmsnorm(kv[:, :, 0], k_norm), kv[:, :, 1]

def peer_ffn(h, w_q, subkeys, u, v):
    B, T, D = h.shape
    n = B * T
    nb = -(-n // PEER_BLOCK)
    xf = jnp.pad(h.reshape(n, D), ((0, nb * PEER_BLOCK - n), (0, 0)))

    def one_block(xb):
        q = (xb @ w_q).reshape(PEER_BLOCK, P_HEADS, 2, P_HALF)
        s = jnp.einsum('nhpe,hpke->nhpk', q, subkeys, preferred_element_type=jnp.float32)
        top_s, top_i = lax.top_k(s, P_TOPK)
        cand_s = (top_s[:, :, 0, :, None] + top_s[:, :, 1, None, :]).reshape(PEER_BLOCK, P_HEADS, P_TOPK * P_TOPK)
        cand_i = (top_i[:, :, 0, :, None] * N_KEYS + top_i[:, :, 1, None, :]).reshape(PEER_BLOCK, P_HEADS, P_TOPK * P_TOPK)
        best_s, best_pos = lax.top_k(cand_s, P_TOPK)
        idx = jnp.take_along_axis(cand_i, best_pos, axis=-1)
        g = jax.nn.softmax(best_s, axis=-1).astype(xb.dtype)
        ue = u[idx]
        ve = v[idx]
        a = jax.nn.gelu(jnp.einsum('nd,nhkd->nhk', xb, ue))
        return jnp.einsum('nhk,nhkd->nd', g * a, ve)

    y = lax.map(one_block, xf.reshape(nb, PEER_BLOCK, D))
    return y.reshape(nb * PEER_BLOCK, D)[:n].reshape(B, T, D)

def setup_inputs(seed: int = 0) -> dict:
    key = jax.random.key(seed)
    ks = iter(jax.random.split(key, 48))

    def nrm(shape, scale):
        return jax.random.normal(next(ks), shape, jnp.float32) * scale

    def gain(shape):
        return 1.0 + nrm(shape, 0.05)

    D = D_MODEL
    b_cache = min(B_WINDOW, PAST_LEN)
    return {
        "x_prompt": nrm((BATCH, SEQ, D), 1.0),
        "x_sample": nrm((DEC_BATCH, DEC_SEQ, D), 1.0),
        "c_prompt": nrm((BATCH, D), 1.0),
        "c_sample": nrm((DEC_BATCH, D), 1.0),
        "cache_a_ckv": nrm((N_A, DEC_BATCH, PAST_LEN, KV_LORA), 1.0),
        "cache_a_krope": nrm((N_A, DEC_BATCH, PAST_LEN, ROPE_DIM), 1.0),
        "cache_b_k": nrm((DEC_BATCH, b_cache, B_HEADS, B_HEAD_DIM), 1.0),
        "cache_b_v": nrm((DEC_BATCH, b_cache, B_HEADS, B_HEAD_DIM), 1.0),
        "ada_w": nrm((DEPTH, D, 6 * D), 0.5 * D ** -0.5),
        "ada_b": nrm((DEPTH, 6 * D), 0.02),
        "norm_mix_w": gain((DEPTH, D)),
        "norm_ffn_w": gain((DEPTH, D)),
        "a_w_in": nrm((N_A, D, Q_LORA + KV_LORA + ROPE_DIM), D ** -0.5),
        "a_q_lora_norm": gain((N_A, Q_LORA)),
        "a_kv_lora_norm": gain((N_A, KV_LORA)),
        "a_w_uq": nrm((N_A, Q_LORA, A_HEADS * QK_DIM), Q_LORA ** -0.5),
        "a_w_ukv": nrm((N_A, KV_LORA, A_HEADS * (NOPE_DIM + V_DIM)), KV_LORA ** -0.5),
        "a_q_norm": gain((N_A, QK_DIM)),
        "a_k_norm": gain((N_A, QK_DIM)),
        "a_w_o": nrm((N_A, A_HEADS * V_DIM, D), (A_HEADS * V_DIM) ** -0.5),
        "kv_ada_w": nrm((D, 2 * D), 0.5 * D ** -0.5),
        "kv_ada_b": nrm((2 * D,), 0.02),
        "kv_norm_w": gain((D,)),
        "b_w_kv": nrm((D, 2 * B_HEADS * B_HEAD_DIM), D ** -0.5),
        "b_k_norm": gain((B_HEAD_DIM,)),
        "b_w_q": nrm((N_B, D, B_HEADS * B_HEAD_DIM), D ** -0.5),
        "b_q_norm": gain((N_B, B_HEAD_DIM)),
        "b_rel_bias": nrm((N_B, B_HEADS, 2 * REL_CLIP + 1), 0.5),
        "b_w_o": nrm((N_B, B_HEADS * B_HEAD_DIM, D), (B_HEADS * B_HEAD_DIM) ** -0.5),
        "p_w_q": nrm((DEPTH, D, P_HEADS * P_DKEY), D ** -0.5),
        "p_subkeys": nrm((DEPTH, P_HEADS, 2, N_KEYS, P_HALF), P_HALF ** -0.5),
        "p_u": nrm((DEPTH, N_EXPERTS, D), D ** -0.5),
        "p_v": nrm((DEPTH, N_EXPERTS, D), P_HEADS ** -0.5),
    }

def reference(x_prompt, x_sample, c_prompt, c_sample, cache_a_ckv, cache_a_krope, cache_b_k, cache_b_v,
              ada_w, ada_b, norm_mix_w, norm_ffn_w,
              a_w_in, a_q_lora_norm, a_kv_lora_norm, a_w_uq, a_w_ukv, a_q_norm, a_k_norm, a_w_o,
              kv_ada_w, kv_ada_b, kv_norm_w, b_w_kv, b_k_norm,
              b_w_q, b_q_norm, b_rel_bias, b_w_o,
              p_w_q, p_subkeys, p_u, p_v):

    def run(x, c, pos, past_ckv, past_kr, past_bk, past_bv):
        prompt = past_bk is None
        new_ckv, new_kr = [], []
        k_all = v_all = k_pos = new_bk = new_bv = None
        for layer in range(DEPTH):
            mod = jax.nn.silu(c) @ ada_w[layer] + ada_b[layer]
            sh_m, sc_m, g_m, sh_f, sc_f, g_f = jnp.split(mod, 6, axis=-1)
            h = modulate(x, norm_mix_w[layer], sh_m, sc_m)
            if layer < N_A:
                i = layer
                out, ckv, kr = mla_mixer(h, pos,
                                         None if prompt else past_ckv[i],
                                         None if prompt else past_kr[i],
                                         a_w_in[i], a_q_lora_norm[i], a_kv_lora_norm[i],
                                         a_w_uq[i], a_w_ukv[i], a_q_norm[i], a_k_norm[i], a_w_o[i])
                new_ckv.append(ckv)
                new_kr.append(kr)
            else:
                j = layer - N_A
                out = band_mixer(h, pos, k_all, v_all, k_pos, b_w_q[j], b_q_norm[j], b_rel_bias[j], b_w_o[j], prompt)
            x = x + g_m[:, None, :] * out
            h = modulate(x, norm_ffn_w[layer], sh_f, sc_f)
            x = x + g_f[:, None, :] * peer_ffn(h, p_w_q[layer], p_subkeys[layer], p_u[layer], p_v[layer])
            if layer == N_A - 1:
                k_new, v_new = shared_kv(x, c, kv_ada_w, kv_ada_b, kv_norm_w, b_w_kv, b_k_norm)
                if prompt:
                    k_all, v_all, k_pos = k_new, v_new, pos
                    new_bk, new_bv = k_new[:, -B_WINDOW:], v_new[:, -B_WINDOW:]
                else:
                    P = past_ckv.shape[2]
                    Pb = past_bk.shape[1]
                    k_all = jnp.concatenate([past_bk, k_new], axis=1)
                    v_all = jnp.concatenate([past_bv, v_new], axis=1)
                    k_pos = jnp.concatenate([P - Pb + jnp.arange(Pb, dtype=jnp.int32), pos])
                    new_bk, new_bv = k_all[:, -Pb:], v_all[:, -Pb:]
        return x, jnp.stack(new_ckv), jnp.stack(new_kr), new_bk, new_bv

    T_p = x_prompt.shape[1]
    T_s = x_sample.shape[1]
    P = cache_a_ckv.shape[2]
    pos_p = jnp.arange(T_p, dtype=jnp.int32)
    pos_s = P + jnp.arange(T_s, dtype=jnp.int32)
    y_prompt, p_ckv, p_kr, p_bk, p_bv = run(x_prompt, c_prompt, pos_p, None, None, None, None)
    y_sample, s_ckv, s_kr, s_bk, s_bv = run(x_sample, c_sample, pos_s, cache_a_ckv, cache_a_krope, cache_b_k, cache_b_v)
    return (y_prompt, y_sample, p_ckv, p_kr, p_bk, p_bv, s_ckv, s_kr, s_bk, s_bv)


_drawn_inputs = setup_inputs


def setup_inputs(seed=0):
    import zlib

    import numpy as np

    out = dict(_drawn_inputs(seed))
    spreads = {}
    factors = {'cache_a_krope': 3.75,
     'norm_ffn_w': 2.802,
     'a_q_lora_norm': 8.0,
     'a_q_norm': 8.0,
     'a_k_norm': 8.0,
     'b_q_norm': 8.0,
     'b_rel_bias': 2.943}
    for name, (base, spread) in spreads.items():
        noise = np.random.default_rng([zlib.crc32(name.encode()), seed]).standard_normal(out[name].shape)
        drawn = base * np.exp(spread * noise) if base else spread * noise
        out[name] = __import__('jax').numpy.asarray(drawn.astype(out[name].dtype))
    for name, factor in factors.items():
        out[name] = (out[name] * factor).astype(out[name].dtype)
    return out
```

```python
from contextlib import ExitStack

import numpy as np

import concourse.bass as bass
from concourse import mybir

F32 = mybir.dt.float32
U32 = mybir.dt.uint32
ALU = mybir.AluOpType
ACT = mybir.ActivationFunctionType
AX = mybir.AxisListType

D = 1024
C = D // 128
SEQ = 512
DEC = 64
PAST = 256
CHUNK = 64
HEADS = 16
Q_LORA = 384
KV_LORA = 256
NOPE = 64
ROPE = 32
HALF = ROPE // 2
QK = NOPE + ROPE
VD = 64
LAT = Q_LORA + KV_LORA + ROPE
BD = 64
REL = 128
PH = 8
NKEYS = 128
TOPK = 16
NEG = -1e30
LOWEST = -3.0e38
EPS = 1e-6
TILES = 5
PT = SEQ // 128
ROWS = [128] * PT + [DEC]
MODS = 14
ADA_BLOCK = 512
ADA_BLOCKS = MODS * D // ADA_BLOCK
SLOTS = 8
GROUP = 2
GROUPS = SLOTS // GROUP
EXPERTS = PH * TOPK
SEGMENTS = [1, 1, 1, 1, 2, 2, 2, 2, 2, 1, 1]
STEPS = EXPERTS // SLOTS
assert sum(SEGMENTS) == STEPS
STARTS = [sum(SEGMENTS[:k]) for k in range(len(SEGMENTS))]
STRIP = 512
EXT = 640


def seq_of(t):
    return 0 if t < PT else 1


def build(nc, a, o):
    ctx = ExitStack()
    with ctx:
        def sb(name, n, parts=128, dt=F32):
            return ctx.enter_context(nc.sbuf_tensor(name, [parts, n], dt))

        sem_names = {}

        def sem(name):
            if name not in sem_names:
                sem_names[name] = ctx.enter_context(nc.semaphore(name))
            return sem_names[name]

        X = sb("X", TILES * D)
        G = sb("G", 2 * D)
        S = sb("S", SLOTS * 2 * D)
        W = sb("W", 18176)
        T1 = sb("T1", 2048)
        qn_r = sb("qn_r", HEADS * QK)
        kn_r = sb("kn_r", HEADS * QK)
        qT_r = sb("qT_r", HEADS * 128)
        hT_r = sb("hT_r", D)
        lat_r = sb("lat_r", LAT)
        latT_r = sb("latT_r", 5 * 128)
        ident = sb("ident", 128)
        zero = sb("zero", 1)
        eps = sb("eps", 1)
        rope = sb("rope", PT * ROPE)
        rows_r = sb("rows_r", Q_LORA + KV_LORA)
        qkw = sb("qkw", 2 * QK)
        modT = sb("modT", 2 * MODS * C)
        normw = sb("normw", 5 * C)
        gain = sb("gain", 2 * 5 * C)
        iota = sb("iota", TOPK)
        masks = sb("masks", 128 + CHUNK)
        stat = sb("stat", 64)
        cT = sb("cT", 3 * 2 * C)
        dots = sb("dots", 4 * SLOTS)
        stage = sb("stage", SLOTS, dt=U32)
        P = ctx.enter_context(nc.psum_tensor("P", [128, 8, 512], F32))

        xt = [X[:, t * D:(t + 1) * D] for t in range(TILES)]
        hT = hT_r[:, :].rearrange("p (c n) -> p c n", c=C)
        xn = T1[:, 0:D]
        ada_bias = S[0:2, 0:MODS * D]
        ada_w = [W[:, b * 4096:(b + 1) * 4096].rearrange("p (c n) -> p c n", c=C) for b in range(4)]
        csT = cT[:, 2 * 2 * C:3 * 2 * C].rearrange("p (c s) -> p c s", s=2)
        w_in = W[:, 0:C * LAT].rearrange("p (c n) -> p c n", c=C)
        w_uq = W[:, C * LAT:C * LAT + 3 * HEADS * QK].rearrange("p (c n) -> p c n", c=3)
        w_oA = W[:, 9984:9984 + C * D].rearrange("p (c n) -> p c n", c=C)
        KTa = S[:, 0:HEADS * SEQ].rearrange("p (h s) -> p h s", h=HEADS)
        Va = S[:, 8192:8192 + 4 * D].rearrange("p (t n) -> p t n", t=4)
        w_ukv = S[:, 12288:16384].rearrange("p (c n) -> p c n", c=2)
        lat = lat_r
        latT = latT_r[:, :].rearrange("p (c n) -> p c n", c=5)
        qT = qT_r[:, :].rearrange("p (h n) -> p h n", h=HEADS)
        probs = [T1[:, 1024 + 512 * b:1536 + 512 * b] for b in range(2)]
        probT = [kn_r[:, 512 * b:512 + 512 * b].rearrange("p (b n) -> p b n", n=128) for b in range(2)]
        Osb = qn_r[:, 0:D]
        oT = hT
        w_kv = W[:, 0:C * 2 * D].rearrange("p (c n) -> p c n", c=C)
        w_q = W[:, 0:C * D].rearrange("p (c n) -> p c n", c=C)
        w_oB = W[:, 8192:8192 + C * D].rearrange("p (c n) -> p c n", c=C)
        KTp = S[:, 0:4096].rearrange("p (c s) -> p c s", c=C)
        Vp = S[:, 4096:8192].rearrange("p (t n) -> p t n", t=4)
        KTs = S[:, 8192:8192 + C * 320].rearrange("p (c s) -> p c s", c=C)
        Vs = S[:, 10752:10752 + 3 * D].rearrange("p (t n) -> p t n", t=3)
        strips = [S[:, 13824 + STRIP * b:13824 + STRIP * (b + 1)] for b in range(2)]
        reverse = S[:, 14848:14976]
        qTb = qT_r[:, 0:D].rearrange("p (c n) -> p c n", c=C)
        w_pq = w_q
        FT = 8192
        cand = W[:, FT:FT + 2048]
        hot = W[:, FT + 2048:FT + 4096]
        hrow = [W[:, FT + 4096 + D * b:FT + 4096 + D * (b + 1)] for b in range(2)]
        qsb = W[:, FT + 6144:FT + 7168]
        val = W[:, FT + 7168:FT + 7424].rearrange("p (g k) -> p g k", k=TOPK)
        ind = W[:, FT + 7424:FT + 7680].bitcast(U32).rearrange("p (g k) -> p g k", k=TOPK)
        indf = W[:, FT + 7680:FT + 7936].rearrange("p (g k) -> p g k", k=TOPK)
        best = W[:, FT + 7936:FT + 8064].rearrange("p (h k) -> p h k", k=TOPK)
        pos = W[:, FT + 8064:FT + 8192].bitcast(U32).rearrange("p (h k) -> p h k", k=TOPK)
        rest = W[:, FT + 8192:FT + 8448]
        pick = W[:, FT + 8448:FT + 8704].rearrange("p (x k) -> p x k", x=2)
        diag = W[:, FT + 8704:FT + 9728].rearrange("p (j n) -> p j n", j=SLOTS)
        expert = [W[:, FT + 9728 + 128 * b:FT + 9856 + 128 * b].bitcast(U32) for b in range(2)]
        gate = [lat_r[:, 128 * b:128 * b + 128] for b in range(2)]
        soft = lat_r[:, 256:384]
        qTp = qTb
        skT = qn_r[:, 0:D].rearrange("p (h k) -> p h k", h=PH)
        slot = [S[:, 2 * D * b:2 * D * (b + 1)] for b in range(SLOTS)]
        score_bank = [0, 1, 4, 5]
        Y = P[:, 6:8, :]

        modTv = modT[:, :].rearrange("p (s j c) -> p s j c", s=2, j=MODS)
        gainv = gain[:, :].rearrange("p (s n c) -> p s n c", s=2, n=5)
        normv = normw[:, :].rearrange("p (n c) -> p n c", n=5)
        Gv = G[:, :].rearrange("p (s n) -> p s n", s=2)
        SHIFT = {"mix0": 0, "ffn0": 3, "mix1": 6, "ffn1": 9, "kv": 12}
        SCALE = {k: v + 1 for k, v in SHIFT.items()}
        GATE = {"mix0": 2, "ffn0": 5, "mix1": 8, "ffn1": 11}
        NORM = {"mix0": 0, "mix1": 1, "ffn0": 2, "ffn1": 3, "kv": 4}
        order = ([("mix0", t) for t in range(TILES)] + [("ffn0", t) for t in range(TILES)]
                 + [("kv", t) for t in range(TILES)] + [("mix1", t) for t in range(TILES)]
                 + [("ffn1", t) for t in range(TILES)])
        norm_at = {x: i for i, x in enumerate(order)}

        KEYS_A = [("new", t) for t in range(PT)] + [("past", 0), ("past", 1), ("new", PT)]
        key_at = {x: i for i, x in enumerate(KEYS_A)}

        mod_dram = nc.dram_tensor("mod_scratch", (2, MODS, D), F32).ap()

        def unit(layer, t):
            return layer * TILES + t

        def keys_of(t):
            return 128 * (t + 1) if t < PT else PAST + DEC

        def blocks_of(t):
            n = keys_of(t)
            return [min(128, n - s) for s in range(0, n, 128)]

        def wait_alone(eng, name, value, passed):
            eng.wait_ge(sem(name), value)
            eng.sem_inc(sem(passed), 1)

        class Chain:

            def __init__(self, eng, name):
                self.eng, self.sem, self.n = eng, sem(name), 0

            def __call__(self, ins):
                self.n += 1
                ins.then_inc(self.sem, 1)
                self.eng.wait_ge(self.sem, self.n)

        block = ctx.enter_context(nc.Block())

        @block.sync
        def _(sp):
            def load(dst, src, name, **kw):
                sp.dma_start(dst, src, **kw).then_inc(sem(name), 16)

            load(cT[:, 0:2 * C].rearrange("p (s c) -> p s c", s=2), a["c"].rearrange("s (p c) -> p s c", c=C), "c_loaded")
            load(ada_bias, a["ada_b"].partition_broadcast(2), "bias_loaded")
            load(ident[:, :], a["ident"], "const_loaded")
            load(iota[:, :], a["iota"], "const_loaded")
            load(rope[:, :], a["rope"], "const_loaded")
            load(masks[:, :], a["masks"], "const_loaded")
            load(normv, a["norms"].rearrange("n (p c) -> p n c", c=C), "const_loaded")
            load(rows_r[:, :], a["lora"].partition_broadcast(128), "const_loaded")
            load(qkw[:, :], a["qkw"].partition_broadcast(128), "const_loaded")
            for t in range(TILES):
                src = a["xp"][t * 128:(t + 1) * 128, :] if t < PT else a["xs"]
                load(xt[t][0:ROWS[t], :], src, "x_loaded")
            with sp.Fori(0, ADA_BLOCKS // 4) as r:
                for b in range(4):
                    sp.wait_ge(sem("ada_freed"), r * 4 + b + 1)
                    sp.dma_start(ada_w[b], a["ada_w"][bass.ds(r * 4 + b, 1), :, :].rearrange("a p (c n) -> (a p) c n", c=C)).then_inc(sem(f"ada_w{b}_loaded"), 16)
            sp.wait_ge(sem("mods_summed"), ADA_BLOCKS + 4)
            load(mod_dram.rearrange("s j n -> s (j n)"), ada_bias, "mods_stored")
            sp.wait_ge(sem("mods_stored"), 16)
            for s in range(2):
                for j in range(MODS):
                    load(modTv[:, s, j, :], mod_dram[s, j, :].rearrange("(p c) -> p c", c=C), "modT_loaded")
            load(w_in, a["w_in"].rearrange("(p c) n -> p c n", c=C), "w_in_loaded")
            load(w_uq, a["w_uq"].rearrange("(c p) n -> p c n", c=3), "w_uq_loaded")
            load(w_ukv, a["w_ukv"].rearrange("(c p) n -> p c n", c=2), "w_ukv_loaded")
            for s in range(2):
                load(Gv[:, s, :], mod_dram[s, GATE["mix0"], :].partition_broadcast(128), "gate_rows_loaded")
            load(w_oA, a["w_oA"].rearrange("(c p) n -> p c n", c=C), "w_oA_loaded")
            for t in range(TILES):
                if t == PT:
                    for k in range(2):
                        if k == 0:
                            sp.wait_ge(sem("lat_stored"), 32 * PT)
                            sp.wait_ge(sem("keys_multiplied"), PT)
                            sp.wait_ge(sem("q_multiplied"), PT)
                        sp.wait_ge(sem("keys_normed"), key_at["past", k])
                        sp.wait_ge(sem("keys_multiplied"), key_at["past", k])
                        load(latT[:, 3:5, :], a["past_ckvT"].rearrange("(c p) n -> p c n", c=2)[:, :, k * 128:(k + 1) * 128], "past_lat_loaded")
                        load(lat[:, 640:672], a["past_kr"][k * 128:(k + 1) * 128, :], "past_lat_loaded")
                r = ROWS[t]
                sp.wait_ge(sem("latents_normed"), t + 1)
                ckv, kr = (o["ckv_p"][t * 128:(t + 1) * 128, :], o["kr_p"][t * 128:(t + 1) * 128, :]) if t < PT else (o["ckv_s"], o["kr_s"])
                load(ckv, lat[0:r, Q_LORA:Q_LORA + KV_LORA], "lat_stored")
                load(kr, lat[0:r, 640:672], "lat_stored")
            for layer in range(2):
                sp.wait_ge(sem("q_multiplied"), unit(layer, TILES - 1) + 1)
                load(w_pq, a["p_w_q"][layer].rearrange("(p c) n -> p c n", c=C), "w_pq_loaded")
                sp.wait_ge(sem("mixed"), unit(layer, TILES - 1) + 1)
                for s in range(2):
                    load(Gv[:, s, :], mod_dram[s, GATE[f"ffn{layer}"], :].partition_broadcast(128), "gate_rows_loaded")
                load(skT, a["skT"][layer], "skT_loaded")
                if layer == 1:
                    break
                sp.wait_ge(sem("experts_added"), unit(0, TILES - 1) + 1)
                load(w_kv, a["w_kv"].rearrange("(p c) n -> p c n", c=C), "w_kv_loaded")
                load(reverse, a["reverse"], "bqk_loaded")
                load(rows_r[:, 0:2 * BD], a["bqk"].partition_broadcast(128), "bqk_loaded")
                for s in range(2):
                    load(Gv[:, s, :], mod_dram[s, GATE["mix1"], :].partition_broadcast(128), "gate_rows_loaded")
                load(KTs[:, :, 0:PAST], a["past_kT"].rearrange("(c p) n -> p c n", c=C), "past_kv_loaded")
                load(Vs[:, 0:2, :], a["past_v"].rearrange("(t p) n -> p t n", p=128), "past_kv_loaded")
                load(o["bk_s"][0:PAST - DEC, :], a["past_k"][DEC:PAST, :], "kept_past_stored")
                load(o["bv_s"][0:PAST - DEC, :], a["past_v"][DEC:PAST, :], "kept_past_stored")
                for t in range(TILES):
                    r = ROWS[t]
                    sp.wait_ge(sem("bk_normed"), t + 1)
                    dk, dv = (o["bk_p"][t * 128:(t + 1) * 128, :], o["bv_p"][t * 128:(t + 1) * 128, :]) if t < PT else (o["bk_s"][PAST - DEC:, :], o["bv_s"][PAST - DEC:, :])
                    load(dk, kn_r[0:r, 0:D], "bk_stored")
                    sp.wait_ge(sem("bv_copied"), t + 1)
                    load(dv, (Vp[:, t, :] if t < PT else Vs[:, 2, :])[0:r, :], "bv_stored")
                sp.wait_ge(sem("kv_multiplied"), TILES)
                load(w_q, a["w_q"].rearrange("(p c) n -> p c n", c=C), "w_q_loaded")
                load(w_oB, a["w_oB"].rearrange("(c p) n -> p c n", c=C), "w_oB_loaded")
                for n in range(TILES * HEADS):
                    if n >= 2:
                        sp.wait_ge(sem("scores_ready"), TILES * HEADS + n - 1)
                    ext = a["rel_ext"]
                    h = n % HEADS
                    src = bass.AP(tensor=ext.tensor, offset=h * EXT, ap=[[1, 128], [1, STRIP]])
                    load(strips[n % 2], src, f"strip{n % 2}_loaded")
            for t in range(TILES):
                sp.wait_ge(sem("experts_added"), unit(1, t) + 1)
                load(o["y_p"][t * 128:(t + 1) * 128, :] if t < PT else o["y_s"], xt[t][0:ROWS[t], :], "y_stored")
            sp.wait_ge(sem("y_stored"), 16 * TILES)
            sp.wait_ge(sem("bk_stored"), 16 * TILES)
            sp.wait_ge(sem("bv_stored"), 16 * TILES)
            sp.wait_ge(sem("kept_past_stored"), 32)
            sp.wait_ge(sem("lat_stored"), 32 * TILES)

        @block.tensor
        def _(pe):
            nc_t = pe

            def products(out, lhs, rhs, n, chunks, r, first=0):
                for j in range(0, n, 512):
                    m = min(512, n - j)
                    for c in range(chunks):
                        ins = nc_t.matmul(out(j, m), lhs(c), rhs(c, j, m), start=(c == 0), stop=(c == chunks - 1))
                return ins

            def turn_norm(kind, t):
                r = ROWS[t]
                pe.wait_ge(sem("xn_ready"), norm_at[kind, t] + 1)
                for c in range(C):
                    ins = nc_t.transpose(P[:, 6 + c // 4, (c % 4) * 128:(c % 4) * 128 + r] if kind[:3] != "ffn"
                                         else P[:, c // 4, (c % 4) * 128:(c % 4) * 128 + r],
                                         xn[0:r, c:D:C], ident[0:r, 0:r])
                ins.then_inc(sem("xn_turned"), 1)

            def attention(layer, t):
                r, nk, bl = ROWS[t], keys_of(t), blocks_of(t)
                n0 = unit(layer, t) * HEADS

                def scores(h):
                    n = n0 + h
                    if n >= 2:
                        pe.wait_ge(sem("probs_ready"), n - 1)
                    if layer == 0:
                        lhs, rhs = qT[0:QK, h, 0:r], KTa[0:QK, h, 0:nk]
                    else:
                        p0 = 64 * (h % 2)
                        lhs = qTb[p0:p0 + 64, h // 2, 0:r]
                        rhs = (KTp if t < PT else KTs)[p0:p0 + 64, h // 2, 0:nk]
                    bank = P[0:r, n % 2, 0:nk]
                    last = t == PT
                    ins = nc_t.matmul(bank, lhs, rhs, start=True, stop=layer == 0 and last, skip_group_check=True)
                    if layer == 1:
                        m = n - TILES * HEADS
                        off = STRIP - nk if t < PT else 128
                        pe.wait_ge(sem(f"strip{m % 2}_loaded"), 16 * (m // 2 + 1))
                        ins = nc_t.matmul(bank, reverse[:, 0:r], strips[m % 2][:, off:off + nk], start=False, stop=last, skip_group_check=True)
                    if t < PT:
                        ins = nc_t.matmul(P[0:r, n % 2, nk - CHUNK:nk], masks[:, 0:128], masks[:, 128:128 + CHUNK],
                                          start=False, stop=True, skip_group_check=True)
                    ins.then_inc(sem("scores_ready"), 1)

                def turn(h):
                    n = n0 + h
                    pe.wait_ge(sem("probs_ready"), n + 1)
                    if n >= 2:
                        pe.wait_ge(sem("probs_copied"), n - 1)
                    for b, k in enumerate(bl):
                        ins = nc_t.transpose(P[0:k, 2 + n % 2, b * 128:b * 128 + r], probs[n % 2][0:r, b * 128:b * 128 + k], ident[0:r, 0:r])
                    ins.then_inc(sem("probs_turned"), 1)

                def values(h):
                    n = n0 + h
                    pe.wait_ge(sem("probs_copied"), n + 1)
                    V = Va if layer == 0 else (Vp if t < PT else Vs)
                    for b, k in enumerate(bl):
                        ins = nc_t.matmul(P[0:r, 4 + h // 8, (h % 8) * 64:(h % 8) * 64 + 64], probT[n % 2][0:k, b, 0:r],
                                          V[0:k, b, h * 64:h * 64 + 64], start=(b == 0), stop=(b == len(bl) - 1), skip_group_check=True)
                    ins.then_inc(sem("values_summed"), 1)

                for h in range(HEADS + 2):
                    if h < HEADS:
                        scores(h)
                    if 1 <= h <= HEADS:
                        turn(h - 1)
                    if h >= 2:
                        values(h - 2)

            def out_product(layer, t):
                r, u = ROWS[t], unit(layer, t)
                w = w_oA if layer == 0 else w_oB
                pe.wait_ge(sem("heads_scaled"), u + 1)
                for c in range(C):
                    ins = nc_t.transpose(P[:, 6 + c // 4, (c % 4) * 128:(c % 4) * 128 + r], Osb[0:r, c * 128:(c + 1) * 128], ident[0:r, 0:r])
                ins.then_inc(sem("heads_turned"), 1)
                pe.wait_ge(sem("heads_copied"), u + 1)
                pe.wait_ge(sem("w_oA_loaded" if layer == 0 else "w_oB_loaded"), 16)
                ins = products(lambda j, m: P[0:r, 4 + j // 512, 0:m], lambda c: oT[:, c, 0:r], lambda c, j, m: w[:, c, j:j + m], D, C, r)
                ins.then_inc(sem("out_multiplied"), 1)

            pe.wait_ge(sem("c_ready"), 1)
            pe.sem_inc(sem("ada_freed"), 4)
            with pe.Fori(0, ADA_BLOCKS // 4) as g:
                for b in range(4):
                    pe.wait_ge(sem("mods_summed"), g * 4 + b + 1)
                    pe.wait_ge(sem(f"ada_w{b}_loaded"), (g + 1) * 16)
                    for c in range(C):
                        ins = nc_t.matmul(P[0:2, b, :], csT[:, c, :], ada_w[b][:, c, :], start=(c == 0), stop=(c == C - 1))
                    ins.then_inc(sem("ada_freed"), 1)

            def keys_A(kind, k):
                n = key_at[kind, k]
                r = ROWS[k] if kind == "new" else 128
                if kind == "past":
                    pe.wait_ge(sem("past_lat_loaded"), 32 * (k + 1))
                    pe.wait_ge(sem("keysT_copied"), n)
                    pe.wait_ge(sem("mixed"), PT)
                else:
                    pe.wait_ge(sem("w_ukv_loaded"), 16)
                if n:
                    pe.wait_ge(sem("v_copied"), n)
                ins = products(lambda j, m: P[0:r, 4 + j // 512, 0:m], lambda c: latT[:, 3 + c, 0:r], lambda c, j, m: w_ukv[:, c, j:j + m], 2 * D, 2, r)
                ins.then_inc(sem("keys_multiplied"), 1)

            def turn_keys_A(kind, k):
                n = key_at[kind, k]
                r = ROWS[k] if kind == "new" else 128
                pe.wait_ge(sem("keys_normed"), n + 1)
                pe.wait_ge(sem("v_copied"), n + 1)
                kn = kn_r[:, :].rearrange("p (h e) -> p h e", h=HEADS)
                for h in range(HEADS):
                    ins = nc_t.transpose(P[0:QK, 4 + h // 4, (h % 4) * 128:(h % 4) * 128 + r], kn[0:r, h, :], ident[0:r, 0:r])
                ins.then_inc(sem("keys_turned"), 1)

            pe.wait_ge(sem("const_loaded"), 16 * 7)
            for t in range(TILES):
                r = ROWS[t]
                if t == PT:
                    for k in range(2):
                        keys_A("past", k)
                        turn_keys_A("past", k)
                    pe.wait_ge(sem("keysT_copied"), PT + 2)
                turn_norm("mix0", t)
                pe.wait_ge(sem("hT_ready"), norm_at["mix0", t] + 1)
                pe.wait_ge(sem("w_in_loaded"), 16)
                for lo, hi, bank in ((0, Q_LORA, 4), (Q_LORA, LAT, 5)):
                    for c in range(C):
                        ins = nc_t.matmul(P[0:r, bank, 0:hi - lo], hT[:, c, 0:r], w_in[:, c, lo:hi], start=(c == 0), stop=(c == C - 1))
                ins.then_inc(sem("latents_multiplied"), 1)
                pe.wait_ge(sem("latents_normed"), t + 1)
                for c in range(5):
                    ins = nc_t.transpose(P[:, 6 + (c >= 3), (c % 3) * 128:(c % 3) * 128 + r], lat[0:r, c * 128:(c + 1) * 128], ident[0:r, 0:r])
                ins.then_inc(sem("latents_turned"), 1)
                pe.wait_ge(sem("latents_copied"), t + 1)
                pe.wait_ge(sem("w_uq_loaded"), 16)
                ins = products(lambda j, m: P[0:r, j // 512, 0:m], lambda c: latT[:, c, 0:r], lambda c, j, m: w_uq[:, c, j:j + m], HEADS * QK, 3, r)
                ins.then_inc(sem("q_multiplied"), 1)
                keys_A("new", t)
                pe.wait_ge(sem("q_normed"), t + 1)
                qn = qn_r[:, :].rearrange("p (h e) -> p h e", h=HEADS)
                for h in range(HEADS):
                    ins = nc_t.transpose(P[0:QK, h // 4, (h % 4) * 128:(h % 4) * 128 + r], qn[0:r, h, :], ident[0:r, 0:r])
                ins.then_inc(sem("q_turned"), 1)
                turn_keys_A("new", t)
                pe.wait_ge(sem("qT_copied"), t + 1)
                pe.wait_ge(sem("keysT_copied"), key_at["new", t] + 1)
                attention(0, t)
                out_product(0, t)

            def select(layer, t, part):
                r, u = ROWS[t], unit(layer, t)
                if part in (1, 2):
                    b = part - 1
                    pe.wait_ge(sem("w_pq_loaded"), 16 * (layer + 1))
                    for c in range(C):
                        ins = nc_t.matmul(P[0:r, b, :], hT[:, c, 0:r], w_pq[:, c, 512 * b:512 * b + 512], start=(c == 0), stop=(c == C - 1))
                    ins.then_inc(sem("pq_multiplied"), 1)
                    return
                if part == 3:
                    pe.wait_ge(sem("pq_copied"), u + 1)
                    pe.wait_ge(sem("h_row_ready"), u + 1)
                    for c in range(C):
                        ins = nc_t.transpose(P[:, 2 + c // 4, (c % 4) * 128:(c % 4) * 128 + r], qsb[0:r, c * 128:(c + 1) * 128], ident[0:r, 0:r])
                    ins.then_inc(sem("pq_turned"), 1)
                    pe.wait_ge(sem("pqT_copied"), u + 1)
                    pe.wait_ge(sem("skT_loaded"), 16 * (layer + 1))
                    for g in range(2 * PH):
                        h, half = g // 2, g % 2
                        ins = nc_t.matmul(P[0:r, score_bank[2 * (h // 4) + g % 2], (h % 4) * 128:(h % 4) * 128 + 128],
                                          qTp[64 * half:64 * half + 64, h, 0:r], skT[64 * half:64 * half + 64, h, :], start=True, stop=True,
                                          skip_group_check=True)
                    ins.then_inc(sem("key_scores_ready"), 1)
                    return
                turn_norm(f"ffn{layer}", t)
                pe.wait_ge(sem("hT_ready"), norm_at[f"ffn{layer}", t] + 1)
                for c in range(C):
                    ins = nc_t.transpose(P[0:r, 2 + c // 4, (c % 4) * 128:(c % 4) * 128 + 128], hT[:, c, 0:r], ident[:, :])
                ins.then_inc(sem("h_turned_back"), 1)

            def experts(layer, t):
                r, u = ROWS[t], unit(layer, t)
                if u:
                    pe.wait_ge(sem("experts_added"), u)
                for b in range(2):
                    nc_t.matmul(Y[0:r, b, :], ident[:, 0:r], zero[:, 0:1].to_broadcast([128, 512]), start=True, stop=False, skip_group_check=True)
                for seg, steps in enumerate(SEGMENTS):
                    base = u * STEPS + STARTS[seg]
                    with pe.Fori(0, steps) as i:
                        for q in range(GROUPS):
                            wait_alone(pe, "weights_spread", i * GROUPS + (GROUPS * base + q + 1), "pe_passed")
                            for j in range(GROUP):
                                for b in range(2):
                                    ins = nc_t.matmul(Y[0:r, b, :], diag[0:r, GROUP * q + j, 0:r], slot[GROUP * q + j][0:r, D + 512 * b:D + 512 * b + 512],
                                                      start=False, stop=False, skip_group_check=True)
                            ins.then_inc(sem("slots_free"), 1)
                    if seg < 4 and t + 1 < TILES:
                        select(layer, t + 1, seg)
                for b in range(2):
                    ins = nc_t.matmul(Y[0:r, b, :], ident[:, 0:r], zero[:, 0:1].to_broadcast([128, 512]), start=False, stop=True, skip_group_check=True)
                ins.then_inc(sem("experts_summed"), 1)

            pe.sem_inc(sem("slots_free"), GROUPS)
            for part in range(4):
                select(0, 0, part)
            for t in range(TILES):
                experts(0, t)

            for t in range(TILES):
                r = ROWS[t]
                turn_norm("kv", t)
                pe.wait_ge(sem("hT_ready"), norm_at["kv", t] + 1)
                pe.wait_ge(sem("w_kv_loaded"), 16)
                if t:
                    pe.wait_ge(sem("bv_copied"), t)
                ins = products(lambda j, m: P[0:r, j // 512, 0:m], lambda c: hT[:, c, 0:r], lambda c, j, m: w_kv[:, c, j:j + m], 2 * D, C, r)
                ins.then_inc(sem("kv_multiplied"), 1)
                pe.wait_ge(sem("bk_normed"), t + 1)
                if t:
                    pe.wait_ge(sem("bkT_copied"), t)
                for c in range(C):
                    ins = nc_t.transpose(P[:, 4 + c // 4, (c % 4) * 128:(c % 4) * 128 + r], kn_r[0:r, c * 128:(c + 1) * 128], ident[0:r, 0:r])
                ins.then_inc(sem("bk_turned"), 1)
            for t in range(TILES):
                r, u = ROWS[t], unit(1, t)
                turn_norm("mix1", t)
                pe.wait_ge(sem("hT_ready"), norm_at["mix1", t] + 1)
                pe.wait_ge(sem("w_q_loaded"), 16)
                pe.wait_ge(sem("bv_copied"), TILES)
                ins = products(lambda j, m: P[0:r, j // 512, 0:m], lambda c: hT[:, c, 0:r], lambda c, j, m: w_q[:, c, j:j + m], D, C, r)
                ins.then_inc(sem("q_multiplied"), 1)
                pe.wait_ge(sem("q_normed"), u + 1)
                pe.wait_ge(sem("bkT_copied"), TILES)
                for c in range(C):
                    ins = nc_t.transpose(P[:, 2 + c // 4, (c % 4) * 128:(c % 4) * 128 + r], qn_r[0:r, c * 128:(c + 1) * 128], ident[0:r, 0:r])
                ins.then_inc(sem("q_turned"), 1)
                pe.wait_ge(sem("qT_copied"), u + 1)
                pe.wait_ge(sem("bqk_loaded"), 32)
                if t == PT:
                    pe.wait_ge(sem("past_kv_loaded"), 32)
                attention(1, t)
                out_product(1, t)
            for part in range(4):
                select(1, 0, part)
            for t in range(TILES):
                experts(1, t)

        @block.scalar
        def _(act):
            step = Chain(act, "act_steps")

            def squares(kind, t):
                r = ROWS[t]
                i = norm_at[kind, t]
                act.wait_ge(sem("x_loaded"), 16 * TILES)
                if i:
                    act.wait_ge(sem("xn_turned"), i)
                done, count = {"mix0": ("mixed", t), "ffn0": ("mixed", TILES), "kv": ("experts_added", TILES),
                               "mix1": ("mixed", TILES + t), "ffn1": ("mixed", 2 * TILES)}[kind]
                if count:
                    act.wait_ge(sem(done), count)
                step(act.activation(xn[0:r, :], xt[t][0:r, :], ACT.Square, accum_out=stat[0:r, 0:1]))
                act.activation(stat[0:r, 1:2], stat[0:r, 0:1], ACT.Sqrt, scale=1.0 / D, bias=eps[0:r, :]).then_inc(sem("rms_ready"), 1)

            def attention(layer, t):
                r, nk = ROWS[t], keys_of(t)
                for h in range(HEADS):
                    n = unit(layer, t) * HEADS + h
                    act.wait_ge(sem("max_ready"), n + 1)
                    if n >= 2:
                        act.wait_ge(sem("probs_turned"), n - 1)
                    act.activation(probs[n % 2][0:r, 0:nk], P[0:r, n % 2, 0:nk], ACT.Exp, bias=stat[0:r, 16 + n % 2:17 + n % 2],
                                   accum_out=row_sum[0:r, h:h + 1]).then_inc(sem("probs_ready"), 1)

            row_sum = stat[:, 32:48]

            act.wait_ge(sem("c_loaded"), 16)
            act.activation(cT[:, 2 * C:4 * C], cT[:, 0:2 * C], ACT.Exp, scale=-1.0).then_inc(sem("c_exp"), 1)
            act.wait_ge(sem("eps_ready"), 1)

            def copy_heads(u, r):
                act.wait_ge(sem("heads_turned"), u + 1)
                for b in range(2):
                    ins = act.copy(oT[:, 4 * b:4 * b + 4, 0:r], P[:, 6 + b, :].rearrange("p (c n) -> p c n", c=4)[:, :, 0:r])
                ins.then_inc(sem("heads_copied"), 1)

            def keys_A(kind, k):
                n = key_at[kind, k]
                r = ROWS[k] if kind == "new" else 128
                act.wait_ge(sem("keys_multiplied"), n + 1)
                if n:
                    act.wait_ge(sem("keys_squares_summed"), n)
                act.wait_ge(sem("q_normed"), (k if kind == "new" else PT - 1) + 1)
                act.activation(T1[0:r, 0:512], P[0:r, 4, :], ACT.Square)
                act.activation(T1[0:r, 512:1024], P[0:r, 5, :], ACT.Square).then_inc(sem("keys_squared"), 1)
                vt = (k if k < PT else 2) if kind == "new" else k
                if kind == "past" and k == 0:
                    act.wait_ge(sem("values_summed"), HEADS * PT)
                act.copy(Va[0:r, vt, 0:512], P[0:r, 6, :])
                act.copy(Va[0:r, vt, 512:1024], P[0:r, 7, :]).then_inc(sem("v_copied"), 1)
                act.wait_ge(sem("keys_squares_summed"), n + 1)
                act.activation(stat[0:r, 48:64], stat[0:r, 32:48], ACT.Sqrt, scale=1.0 / QK, bias=eps[0:r, :]).then_inc(sem("keys_rms"), 1)

            for t in range(TILES):
                r = ROWS[t]
                if t == PT:
                    keys_A("past", 0)
                    keys_A("past", 1)
                squares("mix0", t)
                act.wait_ge(sem("latents_multiplied"), t + 1)
                act.activation(T1[0:r, 0:Q_LORA], P[0:r, 4, 0:Q_LORA], ACT.Square, accum_out=stat[0:r, 2:3])
                step(act.activation(T1[0:r, 512:512 + KV_LORA], P[0:r, 5, 0:KV_LORA], ACT.Square, accum_out=stat[0:r, 3:4]))
                act.activation(stat[0:r, 4:5], stat[0:r, 2:3], ACT.Sqrt, scale=1.0 / Q_LORA, bias=eps[0:r, :])
                act.activation(stat[0:r, 5:6], stat[0:r, 3:4], ACT.Sqrt, scale=1.0 / KV_LORA, bias=eps[0:r, :]).then_inc(sem("latents_rms"), 1)
                act.wait_ge(sem("latents_turned"), t + 1)
                act.copy(latT[:, 0:3, 0:r], P[:, 6, 0:384].rearrange("p (c n) -> p c n", c=3)[:, :, 0:r])
                act.copy(latT[:, 3:5, 0:r], P[:, 7, 0:256].rearrange("p (c n) -> p c n", c=2)[:, :, 0:r]).then_inc(sem("latents_copied"), 1)
                act.wait_ge(sem("q_multiplied"), t + 1)
                for b in range(3):
                    ins = act.activation(T1[0:r, 512 * b:512 * (b + 1)], P[0:r, b, :], ACT.Square)
                ins.then_inc(sem("q_squared"), 1)
                act.wait_ge(sem("q_squares_summed"), t + 1)
                act.activation(stat[0:r, 48:64], stat[0:r, 32:48], ACT.Sqrt, scale=1.0 / QK, bias=eps[0:r, :]).then_inc(sem("q_rms"), 1)
                keys_A("new", t)
                act.wait_ge(sem("q_turned"), t + 1)
                for b in range(4):
                    ins = act.copy(qT[0:QK, 4 * b:4 * b + 4, 0:r], P[0:QK, b, :].rearrange("p (c n) -> p c n", c=4)[:, :, 0:r])
                ins.then_inc(sem("qT_copied"), 1)
                act.wait_ge(sem("keys_normed"), key_at["new", t] + 1)
                attention(0, t)
                copy_heads(t, r)

            def select(layer, t, part):
                r, u = ROWS[t], unit(layer, t)
                if part == 0:
                    squares(f"ffn{layer}", t)
                    act.wait_ge(sem("h_turned_back"), u + 1)
                    for b in range(2):
                        ins = act.copy(hrow[u % 2][0:r, :].rearrange("n (p c) -> n c p", c=C)[:, 4 * b:4 * b + 4, :],
                                       P[0:r, 2 + b, :].rearrange("n (c p) -> n c p", c=4))
                    ins.then_inc(sem("h_row_ready"), 1)
                    return
                if part == 1:
                    return
                b = part - 2
                act.wait_ge(sem("pq_multiplied"), 2 * u + b + 1)
                ins = act.copy(qsb[0:r, 512 * b:512 * b + 512], P[0:r, b, :])
                if part == 2:
                    return
                ins.then_inc(sem("pq_copied"), 1)
                act.wait_ge(sem("pq_turned"), u + 1)
                for b in range(2):
                    ins = act.copy(qTp[:, 4 * b:4 * b + 4, 0:r], P[:, 2 + b, :].rearrange("p (c n) -> p c n", c=4)[:, :, 0:r])
                ins.then_inc(sem("pqT_copied"), 1)

            def choose_exp(layer, t):
                r, u = ROWS[t], unit(layer, t)
                act.wait_ge(sem("best_shifted"), u + 1)
                act.activation(soft[0:r, :], soft[0:r, :], ACT.Exp).then_inc(sem("best_exp"), 1)

            def experts(layer, t):
                r, u = ROWS[t], unit(layer, t)
                for seg, steps in enumerate(SEGMENTS):
                    base = u * STEPS + STARTS[seg]
                    with act.Fori(0, steps) as i:
                        for q in range(GROUPS):
                            act.wait_ge(sem("dots_ready"), i * GROUPS + (GROUPS * base + q + 1))
                            act.activation(dots[0:r, SLOTS + GROUP * q:SLOTS + GROUP * (q + 1)], dots[0:r, GROUP * q:GROUP * (q + 1)],
                                           ACT.Gelu_apprx_tanh).then_inc(sem("gelu_ready"), 1)
                    if t + 1 < TILES:
                        if seg < 4:
                            select(layer, t + 1, seg)
                        if seg == 9:
                            choose_exp(layer, t + 1)

            for part in range(4):
                select(0, 0, part)
            choose_exp(0, 0)
            for t in range(TILES):
                experts(0, t)
            for t in range(TILES):
                r = ROWS[t]
                squares("kv", t)
                act.wait_ge(sem("kv_multiplied"), t + 1)
                for b in range(2):
                    ins = act.activation(T1[0:r, 1024 + 512 * b:1536 + 512 * b], P[0:r, b, :], ACT.Square)
                ins.then_inc(sem("bk_squared"), 1)
                v = Vp[:, t, :] if t < PT else Vs[:, 2, :]
                for b in range(2):
                    ins = act.copy(v[0:r, 512 * b:512 * b + 512], P[0:r, 2 + b, :])
                ins.then_inc(sem("bv_copied"), 1)
                act.wait_ge(sem("bk_squares_summed"), t + 1)
                act.activation(stat[0:r, 48:64], stat[0:r, 32:48], ACT.Sqrt, scale=1.0 / BD, bias=eps[0:r, :]).then_inc(sem("bk_rms"), 1)
            for t in range(TILES):
                r, u = ROWS[t], unit(1, t)
                squares("mix1", t)
                act.wait_ge(sem("q_multiplied"), u + 1)
                for b in range(2):
                    ins = act.activation(T1[0:r, 1024 + 512 * b:1536 + 512 * b], P[0:r, b, :], ACT.Square)
                ins.then_inc(sem("q_squared"), 1)
                act.wait_ge(sem("q_squares_summed"), u + 1)
                act.activation(stat[0:r, 48:64], stat[0:r, 32:48], ACT.Sqrt, scale=1.0 / BD, bias=eps[0:r, :]).then_inc(sem("q_rms"), 1)
                act.wait_ge(sem("q_turned"), u + 1)
                for b in range(2):
                    ins = act.copy(qTb[:, 4 * b:4 * b + 4, 0:r], P[:, 2 + b, :].rearrange("p (c n) -> p c n", c=4)[:, :, 0:r])
                ins.then_inc(sem("qT_copied"), 1)
                attention(1, t)
                copy_heads(u, r)
            for part in range(4):
                select(1, 0, part)
            choose_exp(1, 0)
            for t in range(TILES):
                experts(1, t)

        @block.vector
        def _(dve):
            step = Chain(dve, "dve_steps")
            row_sum = stat[:, 32:48]

            def bc(ap, shape):
                return ap.to_broadcast(shape)

            def normalise(kind, t):
                r, s, i = ROWS[t], seq_of(t), norm_at[kind, t]
                dve.wait_ge(sem("rms_ready"), i + 1)
                step(dve.reciprocal(stat[0:r, 6:7], stat[0:r, 1:2]))
                dve.tensor_scalar(xn[0:r, :], xt[t][0:r, :], stat[0:r, 6:7], None, ALU.mult).then_inc(sem("xn_ready"), 1)
                dve.wait_ge(sem("xn_turned"), i + 1)
                b0 = 0 if kind[:3] == "ffn" else 6
                for c in range(C):
                    ins = dve.tensor_scalar(hT[:, c, 0:r], P[:, b0 + c // 4, (c % 4) * 128:(c % 4) * 128 + r],
                                            gainv[:, s, NORM[kind], c:c + 1], modTv[:, s, SHIFT[kind], c:c + 1], ALU.mult, ALU.add)
                ins.then_inc(sem("hT_ready"), 1)

            def rotate(x, r, tile):
                x1, x2 = x[0:r, :, NOPE:NOPE + HALF], x[0:r, :, NOPE + HALF:QK]
                tab = rope[0:r, tile * ROPE:(tile + 1) * ROPE]
                cos, sin = (bc(tab[:, i * HALF:(i + 1) * HALF].unsqueeze(1), [r, HEADS, HALF]) for i in range(2))
                p = [T1[0:r, 1024 + 256 * i:1280 + 256 * i].rearrange("p (h e) -> p h e", h=HEADS) for i in range(4)]
                dve.tensor_tensor(p[0], x1, cos, ALU.mult)
                dve.tensor_tensor(p[1], x2, sin, ALU.mult)
                dve.tensor_tensor(p[2], x2, cos, ALU.mult)
                step(dve.tensor_tensor(p[3], x1, sin, ALU.mult))
                dve.tensor_tensor(x1, p[0], p[1], ALU.subtract)
                return dve.tensor_tensor(x2, p[2], p[3], ALU.add)

            def scale_heads(layer, t):
                r, u = ROWS[t], unit(layer, t)
                dve.wait_ge(sem("values_summed"), HEADS * (u + 1))
                step(dve.reciprocal(stat[0:r, 48:64], row_sum[0:r, :]))
                for b in range(2):
                    ins = dve.tensor_tensor(Osb[0:r, 512 * b:512 * b + 512].rearrange("p (h e) -> p h e", h=8),
                                            P[0:r, 4 + b, :].rearrange("p (h e) -> p h e", h=8),
                                            bc(stat[0:r, 48 + 8 * b:56 + 8 * b].unsqueeze(2), [r, 8, 64]), ALU.mult)
                ins.then_inc(sem("heads_scaled"), 1)

            def add_mixed(layer, t):
                r, u, s = ROWS[t], unit(layer, t), seq_of(t)
                dve.wait_ge(sem("out_multiplied"), u + 1)
                dve.wait_ge(sem("gate_rows_loaded"), 32 * (2 * layer + 1))
                step(dve.tensor_tensor(T1[0:r, 0:D].rearrange("p (b n) -> p b n", b=2), P[0:r, 4:6, :],
                                       Gv[0:r, s, :].rearrange("p (b n) -> p b n", b=2), ALU.mult))
                ins = dve.tensor_tensor(xt[t][0:r, :], xt[t][0:r, :], T1[0:r, 0:D], ALU.add)
                ins.then_inc(sem("mixed"), 1)
                dve.wait_ge(sem("mixed"), u + 1)

            def attention(layer, t):
                r, nk, bl = ROWS[t], keys_of(t), blocks_of(t)

                def largest(h):
                    n = unit(layer, t) * HEADS + h
                    dve.wait_ge(sem("scores_ready"), n + 1)
                    if n >= 2:
                        dve.wait_ge(sem("probs_ready"), n - 1)
                    dve.tensor_reduce(stat[0:r, 16 + n % 2:17 + n % 2], P[0:r, n % 2, 0:nk], AX.X, ALU.max, negate=True)\
                       .then_inc(sem("max_ready"), 1)

                def copy_probs(h):
                    n = unit(layer, t) * HEADS + h
                    dve.wait_ge(sem("probs_turned"), n + 1)
                    if n >= 2:
                        dve.wait_ge(sem("values_summed"), n - 1)
                    full = sum(k == 128 for k in bl)
                    src = P[:, 2 + n % 2, :].rearrange("p (b n) -> p b n", n=128)
                    ins = dve.tensor_copy(probT[n % 2][:, 0:full, 0:r], src[:, 0:full, 0:r])
                    if full < len(bl):
                        ins = dve.tensor_copy(probT[n % 2][0:bl[-1], full, 0:r], src[0:bl[-1], full, 0:r])
                    ins.then_inc(sem("probs_copied"), 1)

                for h in range(HEADS + 1):
                    if h < HEADS:
                        largest(h)
                    if h >= 1:
                        copy_probs(h - 1)

            dve.memset(zero[:, :], 0.0)
            dve.memset(eps[:, :], EPS).then_inc(sem("eps_ready"), 1)
            dve.wait_ge(sem("c_exp"), 1)
            step(dve.tensor_scalar(cT[:, 2 * C:4 * C], cT[:, 2 * C:4 * C], 1.0, None, ALU.add))
            step(dve.reciprocal(cT[:, 2 * C:4 * C], cT[:, 2 * C:4 * C]))
            dve.tensor_tensor(csT, cT[:, 0:2 * C].rearrange("p (s c) -> p c s", s=2),
                              cT[:, 2 * C:4 * C].rearrange("p (s c) -> p c s", s=2), ALU.mult).then_inc(sem("c_ready"), 1)
            dve.wait_ge(sem("bias_loaded"), 16)
            dve.sem_inc(sem("mods_summed"), 4)
            with dve.Fori(0, ADA_BLOCKS // 4) as g:
                for b in range(4):
                    dve.wait_ge(sem("ada_freed"), g * 4 + (b + 5))
                    row = ada_bias[:, bass.ds((g * 4 + b) * ADA_BLOCK, ADA_BLOCK)]
                    dve.tensor_tensor(row, P[0:2, b, :], row, ALU.add).then_inc(sem("mods_summed"), 1)
            dve.wait_ge(sem("modT_loaded"), 16 * 2 * MODS)
            dve.wait_ge(sem("const_loaded"), 16 * 7)
            for kind in NORM:
                for s in range(2):
                    dve.scalar_tensor_tensor(gainv[:, s, NORM[kind], :], modTv[:, s, SCALE[kind], :], 1.0, normv[:, NORM[kind], :], ALU.add, ALU.mult)
            step(dve.tensor_scalar(qkw[:, 0:QK], qkw[:, 0:QK], float(QK) ** -0.5, None, ALU.mult))

            def keys_A(kind, k):
                n = key_at[kind, k]
                r = ROWS[k] if kind == "new" else 128
                kn = kn_r[:, :].rearrange("p (h e) -> p h e", h=HEADS)
                dve.wait_ge(sem("keys_squared"), n + 1)
                if kind == "past":
                    dve.wait_ge(sem("past_lat_loaded"), 32 * (k + 1))
                step(dve.tensor_tensor(T1[0:r, 1024:1024 + ROPE], lat[0:r, 640:672], lat[0:r, 640:672], ALU.mult))
                dve.tensor_reduce(stat[0:r, 7:8], T1[0:r, 1024:1024 + ROPE], AX.X, ALU.add)
                step(dve.tensor_reduce(stat[0:r, 32:48], T1[0:r, 0:D].rearrange("p (h e) -> p h e", h=HEADS), AX.X, ALU.add))
                dve.tensor_scalar(stat[0:r, 32:48], stat[0:r, 32:48], stat[0:r, 7:8], None, ALU.add).then_inc(sem("keys_squares_summed"), 1)
                dve.wait_ge(sem("keys_rms"), n + 1)
                step(dve.reciprocal(stat[0:r, 48:64], stat[0:r, 48:64]))
                if n:
                    dve.wait_ge(sem("keys_turned"), n)
                inv = stat[0:r, 48:64].unsqueeze(2)
                for b in range(2):
                    dve.tensor_tensor(kn[0:r, 8 * b:8 * b + 8, 0:NOPE], P[0:r, 4 + b, :].rearrange("p (h e) -> p h e", h=8),
                                      bc(inv[:, 8 * b:8 * b + 8, :], [r, 8, NOPE]), ALU.mult)
                step(dve.tensor_tensor(kn[0:r, :, NOPE:QK], bc(lat[0:r, 640:672].unsqueeze(1), [r, HEADS, ROPE]), bc(inv, [r, HEADS, ROPE]), ALU.mult))
                step(dve.tensor_tensor(kn[0:r, :, :], kn[0:r, :, :], bc(qkw[0:r, QK:2 * QK].unsqueeze(1), [r, HEADS, QK]), ALU.mult))
                tile = (k if k < PT else 2) if kind == "new" else k
                rotate(kn, r, tile).then_inc(sem("keys_normed"), 1)

            def copy_keys_A(kind, k):
                n = key_at[kind, k]
                r = ROWS[k] if kind == "new" else 128
                tile = (k if k < PT else 2) if kind == "new" else k
                dve.wait_ge(sem("keys_turned"), n + 1)
                for b in range(4):
                    ins = dve.tensor_copy(KTa[0:QK, 4 * b:4 * b + 4, tile * 128:tile * 128 + r],
                                          P[0:QK, 4 + b, :].rearrange("p (h n) -> p h n", h=4)[:, :, 0:r])
                ins.then_inc(sem("keysT_copied"), 1)

            for t in range(TILES):
                r = ROWS[t]
                if t == PT:
                    for k in range(2):
                        keys_A("past", k)
                        copy_keys_A("past", k)
                normalise("mix0", t)
                dve.wait_ge(sem("latents_rms"), t + 1)
                step(dve.reciprocal(stat[0:r, 4:6], stat[0:r, 4:6]))
                if t:
                    dve.wait_ge(sem("lat_stored"), 32 * t)
                if t == PT:
                    dve.wait_ge(sem("keys_normed"), PT + 2)
                dve.scalar_tensor_tensor(lat[0:r, 0:Q_LORA], P[0:r, 4, 0:Q_LORA], stat[0:r, 4:5], rows_r[0:r, 0:Q_LORA], ALU.mult, ALU.mult)
                dve.scalar_tensor_tensor(lat[0:r, Q_LORA:640], P[0:r, 5, 0:KV_LORA], stat[0:r, 5:6], rows_r[0:r, Q_LORA:640], ALU.mult, ALU.mult)
                dve.tensor_copy(lat[0:r, 640:672], P[0:r, 5, KV_LORA:KV_LORA + ROPE]).then_inc(sem("latents_normed"), 1)
                qn = qn_r[:, :].rearrange("p (h e) -> p h e", h=HEADS)
                dve.wait_ge(sem("q_squared"), t + 1)
                dve.tensor_reduce(stat[0:r, 32:48], T1[0:r, 0:HEADS * QK].rearrange("p (h e) -> p h e", h=HEADS), AX.X, ALU.add).then_inc(sem("q_squares_summed"), 1)
                dve.wait_ge(sem("q_rms"), t + 1)
                step(dve.reciprocal(stat[0:r, 48:64], stat[0:r, 48:64]))
                step(dve.tensor_tensor(qn[0:r, :, :], P[0:r, 0:3, :].rearrange("p b n -> p (b n)").rearrange("p (h e) -> p h e", h=HEADS),
                                       bc(stat[0:r, 48:64].unsqueeze(2), [r, HEADS, QK]), ALU.mult))
                step(dve.tensor_tensor(qn[0:r, :, :], qn[0:r, :, :], bc(qkw[0:r, 0:QK].unsqueeze(1), [r, HEADS, QK]), ALU.mult))
                rotate(qn, r, t if t < PT else 2).then_inc(sem("q_normed"), 1)
                dve.wait_ge(sem("q_normed"), t + 1)
                keys_A("new", t)
                copy_keys_A("new", t)
                attention(0, t)
                scale_heads(0, t)
                add_mixed(0, t)

            def top16(r, src, values, indices, length, spare):
                step(dve.max(values[:, 0:8], src))
                dve.max_index(indices[:, 0:8], values[:, 0:8], src)
                step(dve.match_replace(spare, values[:, 0:8], src, LOWEST))
                step(dve.max(values[:, 8:16], spare))
                step(dve.max_index(indices[:, 8:16], values[:, 8:16], spare))

            def choose(layer, t, part):
                r, u = ROWS[t], unit(layer, t)
                if part < 4:
                    if part == 0:
                        dve.wait_ge(sem("key_scores_ready"), u + 1)
                    for h in range(2 * part, 2 * part + 2):
                        for g in (2 * h, 2 * h + 1):
                            src = P[0:r, score_bank[2 * (h // 4) + g % 2], (h % 4) * 128:(h % 4) * 128 + 128]
                            top16(r, src, val[0:r, g, :], ind[0:r, g, :], NKEYS, rest[0:r, 0:NKEYS])
                        cd = cand[0:r, h * 256:(h + 1) * 256]
                        step(dve.tensor_tensor(cd.rearrange("p (a b) -> p a b", a=TOPK),
                                               bc(val[0:r, 2 * h, :].unsqueeze(2), [r, TOPK, TOPK]),
                                               bc(val[0:r, 2 * h + 1, :].unsqueeze(1), [r, TOPK, TOPK]), ALU.add))
                        top16(r, cd, best[0:r, h, :], pos[0:r, h, :], 256, rest[0:r, :])
                    return
                x = part - 4
                ch = cand[0:r, :].rearrange("p (g k j) -> p g k j", g=PH, k=TOPK)
                ht = hot[0:r, :].rearrange("p (g k j) -> p g k j", g=PH, k=TOPK)
                if x == 0:
                    pk = pick[0:r, :, :].bitcast(U32)
                    pf = pos[0:r, :, :].rearrange("p h k -> p (h k)")
                    dve.tensor_scalar(pk[:, 0, :], pf, 4, None, ALU.logical_shift_right)
                    step(dve.tensor_scalar(pk[:, 1, :], pf, 15, None, ALU.bitwise_and))
                    dve.tensor_copy(pick[0:r, :, :], pk)
                    step(dve.tensor_copy(indf[0:r, :, :], ind[0:r, :, :]))
                sf = soft[0:r, :].rearrange("p (h k) -> p h k", h=PH)
                if x == 1:
                    dve.tensor_tensor(sf, best[0:r, :, :], bc(best[0:r, :, 0:1], [r, PH, TOPK]), ALU.subtract).then_inc(sem("best_shifted"), 1)
                tab = indf[0:r, x:2 * PH:2, :].unsqueeze(2)
                step(dve.tensor_tensor(ch.rearrange("p g k j -> p (g k) j"),
                                       bc(iota[0:r, :].unsqueeze(1), [r, PH * TOPK, TOPK]),
                                       bc(pick[0:r, x, :].unsqueeze(2), [r, PH * TOPK, TOPK]), ALU.is_equal))
                step(dve.tensor_tensor(ht, ch, bc(tab, [r, PH, TOPK, TOPK]), ALU.mult))
                step(dve.tensor_reduce(hsum[0:r, x, :], ht.rearrange("p g k j -> p (g k) j"), AX.X, ALU.add))
                if x == 0:
                    return
                dve.scalar_tensor_tensor(expert[u % 2][0:r, :], hsum[0:r, 0, :], float(NKEYS), hsum[0:r, 1, :], ALU.mult, ALU.add)
                dve.wait_ge(sem("best_exp"), u + 1)
                step(dve.tensor_reduce(stat[0:r, 24:32], sf, AX.X, ALU.add))
                step(dve.reciprocal(stat[0:r, 24:32], stat[0:r, 24:32]))
                dve.tensor_tensor(gate[u % 2][0:r, :].rearrange("p (h k) -> p h k", h=PH), sf,
                                  bc(stat[0:r, 24:32].unsqueeze(2), [r, PH, TOPK]), ALU.mult).then_inc(sem("experts_chosen"), 1)
                dve.wait_ge(sem("experts_chosen"), u + 1)

            hsum = lat_r[:, 384:640].rearrange("p (x k) -> p x k", x=2)

            def experts(layer, t):
                r, u, s = ROWS[t], unit(layer, t), seq_of(t)
                for seg, steps in enumerate(SEGMENTS):
                    base = u * STEPS + STARTS[seg]
                    with dve.Fori(0, steps) as i:
                        for q in range(GROUPS):
                            for b in range(GROUP * q, GROUP * (q + 1)):
                                dve.wait_ge(sem(f"rows{b}_gathered"), i * 16 + 16 * (base + 1))
                                ins = dve.tensor_tensor_reduce(slot[b][0:r, 0:D], slot[b][0:r, 0:D], hrow[u % 2][0:r, :], 1.0, 0.0,
                                                               ALU.mult, ALU.add, dots[0:r, b:b + 1])
                            ins.then_inc(sem("dots_ready"), 1)
                            nth = i * GROUPS + (GROUPS * base + q + 1)
                            dve.wait_ge(sem("gelu_ready"), nth)
                            wts = dots[0:r, 2 * SLOTS + GROUP * q:2 * SLOTS + GROUP * (q + 1)]
                            dve.tensor_tensor(wts, dots[0:r, SLOTS + GROUP * q:SLOTS + GROUP * (q + 1)],
                                              gate[u % 2][0:r, bass.ds(i * SLOTS + (STARTS[seg] * SLOTS + GROUP * q), GROUP)],
                                              ALU.mult).then_inc(sem("weights_ready"), 1)
                            dve.wait_ge(sem("weights_ready"), nth)
                            dve.tensor_tensor(diag[0:r, GROUP * q:GROUP * (q + 1), 0:r], bc(ident[0:r, 0:r].unsqueeze(1), [r, GROUP, r]),
                                              bc(wts.unsqueeze(2), [r, GROUP, r]), ALU.mult).then_inc(sem("weights_spread"), 1)
                    if t + 1 < TILES:
                        if seg == 0:
                            normalise(f"ffn{layer}", t + 1)
                        if 4 <= seg < 10:
                            choose(layer, t + 1, seg - 4)
                dve.wait_ge(sem("experts_summed"), u + 1)
                if t == 0:
                    dve.wait_ge(sem("gate_rows_loaded"), 32 * (2 * layer + 2))
                step(dve.tensor_tensor(hot[0:r, 0:D].rearrange("p (b n) -> p b n", b=2), Y[0:r, :, :],
                                       Gv[0:r, s, :].rearrange("p (b n) -> p b n", b=2), ALU.mult))
                dve.tensor_tensor(xt[t][0:r, :], xt[t][0:r, :], hot[0:r, 0:D], ALU.add).then_inc(sem("experts_added"), 1)

            def mixer(layer):
                normalise(f"ffn{layer}", 0)
                for part in range(6):
                    choose(layer, 0, part)
                for t in range(TILES):
                    experts(layer, t)
                    dve.wait_ge(sem("experts_added"), unit(layer, t) + 1)

            mixer(0)
            dve.wait_ge(sem("experts_added"), TILES)

            def head_norm(r, banks, dst, w, squares, summed, rms, n):
                dve.wait_ge(sem(squares), n + 1)
                dve.tensor_reduce(stat[0:r, 32:48], T1[0:r, D:2 * D].rearrange("p (h e) -> p h e", h=HEADS), AX.X, ALU.add).then_inc(sem(summed), 1)
                dve.wait_ge(sem(rms), n + 1)
                step(dve.reciprocal(stat[0:r, 48:64], stat[0:r, 48:64]))
                for b in range(2):
                    ins = dve.tensor_tensor(dst[0:r, 512 * b:512 * b + 512].rearrange("p (h e) -> p h e", h=8),
                                            P[0:r, banks + b, :].rearrange("p (h e) -> p h e", h=8),
                                            bc(stat[0:r, 48 + 8 * b:56 + 8 * b].unsqueeze(2), [r, 8, BD]), ALU.mult)
                step(ins)
                x = dst[0:r, 0:D].rearrange("p (h e) -> p h e", h=HEADS)
                return dve.tensor_tensor(x, x, bc(w[0:r, :].unsqueeze(1), [r, HEADS, BD]), ALU.mult)

            dve.wait_ge(sem("bqk_loaded"), 32)
            step(dve.tensor_scalar(rows_r[:, 0:BD], rows_r[:, 0:BD], float(BD) ** -0.5, None, ALU.mult))
            for t in range(TILES):
                r = ROWS[t]
                normalise("kv", t)
                if t:
                    dve.wait_ge(sem("bk_stored"), 16 * t)
                head_norm(r, 0, kn_r, rows_r[:, BD:2 * BD], "bk_squared", "bk_squares_summed", "bk_rms", t).then_inc(sem("bk_normed"), 1)
                dve.wait_ge(sem("bk_turned"), t + 1)
                kt, at = (KTp, 128 * t) if t < PT else (KTs, PAST)
                for b in range(2):
                    ins = dve.tensor_copy(kt[:, 4 * b:4 * b + 4, at:at + r], P[:, 4 + b, :].rearrange("p (c n) -> p c n", c=4)[:, :, 0:r])
                ins.then_inc(sem("bkT_copied"), 1)
            for t in range(TILES):
                r, u = ROWS[t], unit(1, t)
                normalise("mix1", t)
                head_norm(r, 0, qn_r, rows_r[:, 0:BD], "q_squared", "q_squares_summed", "q_rms", u).then_inc(sem("q_normed"), 1)
                if t == 0:
                    dve.wait_ge(sem("bk_stored"), 16 * TILES)
                attention(1, t)
                scale_heads(1, t)
                add_mixed(1, t)
            mixer(1)

        @block.gpsimd
        def _(pool):
            for layer in range(2):
                for t in range(TILES):
                    r, u = ROWS[t], unit(layer, t)
                    table = a[f"uv{layer}"]
                    pool.wait_ge(sem("experts_chosen"), u + 1)
                    for seg, steps in enumerate(SEGMENTS):
                        base = u * STEPS + STARTS[seg]
                        with pool.Fori(0, steps) as i:
                            for q in range(GROUPS):
                                nth = i * GROUPS + (GROUPS * base + q + 1)
                                wait_alone(pool, "slots_free", nth, "pool_passed")
                                cols = slice(GROUP * q, GROUP * (q + 1))
                                pool.tensor_copy(stage[0:r, cols], expert[u % 2][0:r, bass.ds(i * SLOTS + (STARTS[seg] * SLOTS + GROUP * q), GROUP)])\
                                    .then_inc(sem("indices_staged"), 1)
                                wait_alone(pool, "indices_staged", nth, "pool_passed")
                                for b in range(GROUP * q, GROUP * (q + 1)):
                                    pool.indirect_dma_start(slot[b][0:r, :], None, table,
                                                            bass.IndirectOffsetOnAxis(ap=stage[0:r, b:b + 1], axis=0)).then_inc(sem(f"rows{b}_gathered"), 16)


def program(nc, ins, outs):
    ins = {k: nc.dram_tensor(f"in_{k}", v, F32, kind="ExternalInput").ap() for k, v in ins.items()}
    outs = {k: nc.dram_tensor(f"out_{k}", v, F32, kind="ExternalOutput").ap() for k, v in outs.items()}
    build(nc, ins, outs)


def kernel(x_prompt, x_sample, c_prompt, c_sample, cache_a_ckv, cache_a_krope, cache_b_k, cache_b_v,
           ada_w, ada_b, norm_mix_w, norm_ffn_w, a_w_in, a_q_lora_norm, a_kv_lora_norm, a_w_uq, a_w_ukv,
           a_q_norm, a_k_norm, a_w_o, kv_ada_w, kv_ada_b, kv_norm_w, b_w_kv, b_k_norm, b_w_q, b_q_norm,
           b_rel_bias, b_w_o, p_w_q, p_subkeys, p_u, p_v):
    import concourse.bacc as bacc
    from concourse.bass_utils import run_bass_kernel_spmd

    f = lambda x: np.ascontiguousarray(np.asarray(x))
    pos = np.arange(SEQ, dtype=np.float32)
    freqs = (np.float32(10000.0) ** (-np.arange(HALF, dtype=np.float32) / HALF)).astype(np.float32)
    ang = pos[:, None] * freqs[None, :]
    rope = np.concatenate([np.cos(ang), np.sin(ang)], axis=1).astype(np.float32)
    rope = rope.reshape(PT, 128, ROPE).transpose(1, 0, 2).reshape(128, PT * ROPE)
    masks = np.zeros((128, 128 + CHUNK), np.float32)
    masks[0, 0:CHUNK] = 1.0
    masks[0, 128:] = NEG
    ada = np.concatenate([f(ada_w)[0], f(ada_w)[1], f(kv_ada_w)], axis=1)
    ada = ada.reshape(128, C, ADA_BLOCKS, ADA_BLOCK).transpose(2, 0, 1, 3).reshape(ADA_BLOCKS, 128, C * ADA_BLOCK)
    ukv = f(a_w_ukv)[0].reshape(KV_LORA, HEADS, 2, 64).transpose(0, 2, 1, 3).reshape(KV_LORA, 2 * D)
    rel = f(b_rel_bias)[0]
    ext = np.concatenate([np.repeat(rel[:, 256:257], 384, axis=1), rel[:, 255:0:-1], rel[:, 0:1]], axis=1)
    arrays = {
        "xp": f(x_prompt)[0], "xs": f(x_sample)[0], "c": np.concatenate([f(c_prompt), f(c_sample)], axis=0),
        "ada_w": ada, "ada_b": np.concatenate([f(ada_b)[0], f(ada_b)[1], f(kv_ada_b)]),
        "norms": np.concatenate([f(norm_mix_w), f(norm_ffn_w), f(kv_norm_w)[None]], axis=0),
        "lora": np.concatenate([f(a_q_lora_norm)[0], f(a_kv_lora_norm)[0]]),
        "qkw": np.concatenate([f(a_q_norm)[0], f(a_k_norm)[0]]),
        "bqk": np.concatenate([f(b_q_norm)[0], f(b_k_norm)]),
        "w_in": f(a_w_in)[0], "w_uq": f(a_w_uq)[0], "w_ukv": ukv, "w_oA": f(a_w_o)[0],
        "past_ckvT": f(cache_a_ckv)[0, 0].T, "past_kr": f(cache_a_krope)[0, 0],
        "past_k": f(cache_b_k)[0].reshape(PAST, D), "past_v": f(cache_b_v)[0].reshape(PAST, D),
        "past_kT": f(cache_b_k)[0].reshape(PAST, D).T,
        "w_kv": f(b_w_kv), "w_q": f(b_w_q)[0], "w_oB": f(b_w_o)[0], "p_w_q": f(p_w_q),
        "rel_ext": ext,
        "skT": f(p_subkeys).transpose(0, 2, 4, 1, 3).reshape(2, 128, PH, NKEYS),
        "uv0": np.concatenate([f(p_u)[0], f(p_v)[0]], axis=1), "uv1": np.concatenate([f(p_u)[1], f(p_v)[1]], axis=1),
        "ident": np.eye(128, dtype=np.float32), "reverse": np.eye(128, dtype=np.float32)[::-1], "iota": np.tile(np.arange(TOPK, dtype=np.float32), (128, 1)),
        "rope": rope, "masks": masks,
    }
    arrays = {k: np.ascontiguousarray(v) for k, v in arrays.items()}
    shapes = {"y_p": (SEQ, D), "y_s": (DEC, D), "ckv_p": (SEQ, KV_LORA), "kr_p": (SEQ, ROPE), "bk_p": (SEQ, D), "bv_p": (SEQ, D),
              "ckv_s": (DEC, KV_LORA), "kr_s": (DEC, ROPE), "bk_s": (PAST, D), "bv_s": (PAST, D)}
    nc = bacc.Bacc("TRN2", target_bir_lowering=False, num_devices=1)
    program(nc, {k: v.shape for k, v in arrays.items()}, shapes)
    res = run_bass_kernel_spmd(nc, [{f"in_{k}": v for k, v in arrays.items()}], core_ids=[0]).results[0]
    g = {k: res[f"out_{k}"] for k in shapes}
    return (g["y_p"][None], g["y_s"][None], g["ckv_p"][None, None], g["kr_p"][None, None],
            g["bk_p"].reshape(1, SEQ, HEADS, BD), g["bv_p"].reshape(1, SEQ, HEADS, BD),
            g["ckv_s"][None, None], g["kr_s"][None, None],
            g["bk_s"].reshape(1, PAST, HEADS, BD), g["bv_s"].reshape(1, PAST, HEADS, BD))
```

```python
from contextlib import ExitStack

import numpy as np

import concourse.bass as bass
from concourse import mybir

F32 = mybir.dt.float32
U32 = mybir.dt.uint32
ALU = mybir.AluOpType
ACT = mybir.ActivationFunctionType
AX = mybir.AxisListType

D = 1024
C = D // 128
SEQ = 512
DEC = 64
PAST = 256
CHUNK = 64
HEADS = 16
Q_LORA = 384
KV_LORA = 256
NOPE = 64
ROPE = 32
HALF = ROPE // 2
QK = NOPE + ROPE
VD = 64
LAT = Q_LORA + KV_LORA + ROPE
BD = 64
REL = 128
PH = 8
NKEYS = 128
TOPK = 16
NEG = -1e30
LOWEST = -3.0e38
AT_SQUARES, AT_NORM, AT_TURN, AT_GAIN = 6, 8, 10, 12
EPS = 1e-6
TILES = 5
PT = SEQ // 128
ROWS = [128] * PT + [DEC]
MODS = 14
ADA_BLOCK = 512
ADA_BLOCKS = MODS * D // ADA_BLOCK
SLOTS = 8
GROUP = 2
GROUPS = SLOTS // GROUP
EXPERTS = PH * TOPK
SEGMENTS = [[1, 1, 1, 1, 1, 1, 1, 1, 2, 2, 2, 2]] * PT + [[1, 1, 1, 1, 4]]
STEPS = [sum(x) for x in SEGMENTS]
assert STEPS == [EXPERTS // SLOTS] * PT + [EXPERTS // SLOTS // 2]
FIRST = [3] * PT + [4]
SELECT_AT = 4
STRIP = 512


def seq_of(t):
    return 0 if t < PT else 1


def build(nc, a, o):
    ctx = ExitStack()
    with ctx:
        def sb(name, n, parts=128, dt=F32):
            return ctx.enter_context(nc.sbuf_tensor(name, [parts, n], dt))

        sem_names = {}

        def sem(name):
            if name not in sem_names:
                sem_names[name] = ctx.enter_context(nc.semaphore(name))
            return sem_names[name]

        X = sb("X", TILES * D)
        G = sb("G", 2 * D)
        S = sb("S", SLOTS * 2 * D)
        W = sb("W", 18176)
        T1 = sb("T1", 2048)
        qn_r = sb("qn_r", HEADS * QK)
        kn_r = sb("kn_r", HEADS * QK)
        qT_r = sb("qT_r", HEADS * 128)
        hT_r = sb("hT_r", D)
        lat_r = sb("lat_r", LAT)
        latT_r = sb("latT_r", 5 * 128)
        ident = sb("ident", 128)
        zero = sb("zero", 1)
        eps = sb("eps", 1)
        rope = sb("rope", PT * ROPE)
        rows_r = sb("rows_r", Q_LORA + KV_LORA)
        qkw = sb("qkw", 2 * QK)
        modT = sb("modT", 2 * MODS * C)
        normw = sb("normw", 5 * C)
        gain = sb("gain", 2 * 5 * C)
        iota = sb("iota", TOPK)
        masks = sb("masks", 128 + CHUNK)
        stat = sb("stat", 64)
        cT = sb("cT", 3 * 2 * C)
        dots = sb("dots", 4 * SLOTS)
        stage = sb("stage", SLOTS, dt=U32)
        P = ctx.enter_context(nc.psum_tensor("P", [128, 8, 512], F32))

        xt = [X[:, t * D:(t + 1) * D] for t in range(TILES)]
        hT = hT_r[:, :].rearrange("p (c n) -> p c n", c=C)
        xn = T1[:, 0:D]
        ada_bias = S[0:2, 0:MODS * D]
        ada_w = [W[:, b * 4096:(b + 1) * 4096].rearrange("p (c n) -> p c n", c=C) for b in range(4)]
        csT = cT[:, 2 * 2 * C:3 * 2 * C].rearrange("p (c s) -> p c s", s=2)
        w_in = W[:, 0:C * LAT].rearrange("p (c n) -> p c n", c=C)
        w_uq = W[:, C * LAT:C * LAT + 3 * HEADS * QK].rearrange("p (c n) -> p c n", c=3)
        w_oA = W[:, 9984:9984 + C * D].rearrange("p (c n) -> p c n", c=C)
        KTa = S[:, 0:HEADS * SEQ].rearrange("p (h s) -> p h s", h=HEADS)
        Va = S[:, 8192:8192 + 4 * D].rearrange("p (t n) -> p t n", t=4)
        w_ukv = S[:, 12288:16384].rearrange("p (c n) -> p c n", c=2)
        lat = lat_r
        latT = latT_r[:, :].rearrange("p (c n) -> p c n", c=5)
        qT = qT_r[:, :].rearrange("p (h n) -> p h n", h=HEADS)
        probs = [T1[:, 1024 + 512 * b:1536 + 512 * b] for b in range(2)]
        probT = [kn_r[:, 512 * b:512 + 512 * b].rearrange("p (b n) -> p b n", n=128) for b in range(2)]
        turner = [qn_r[:, 128 * b:128 * b + 128] for b in range(2)]
        oT = qT_r[:, 0:D].rearrange("p (c n) -> p c n", c=C)
        w_k = W[:, 0:C * D].rearrange("p (c n) -> p c n", c=C)
        w_v = W[:, C * D:2 * C * D].rearrange("p (c n) -> p c n", c=C)
        w_q = W[:, 0:C * D].rearrange("p (c n) -> p c n", c=C)
        w_oB = W[:, 8192:8192 + C * D].rearrange("p (c n) -> p c n", c=C)
        hT_odd = W[:, C * 2 * D:C * 2 * D + D].rearrange("p (c n) -> p c n", c=C)
        KTp = S[:, 0:4096].rearrange("p (c s) -> p c s", c=C)
        Vp = S[:, 4096:8192].rearrange("p (t n) -> p t n", t=4)
        KTs = S[:, 8192:8192 + C * 320].rearrange("p (c s) -> p c s", c=C)
        Vs = S[:, 10752:10752 + 3 * D].rearrange("p (t n) -> p t n", t=3)
        strips = [S[:, 13824 + STRIP * b:13824 + STRIP * (b + 1)] for b in range(2)]
        biased = [S[:, 14848 + 512 * b:15360 + 512 * b] for b in range(2)]
        qTb = qT_r[:, 0:D].rearrange("p (c n) -> p c n", c=C)
        w_pq = w_q
        FT = 8192
        cand = W[:, FT:FT + 2048]
        hot = W[:, FT + 2048:FT + 4096]
        hrow = [W[:, FT + 4096 + D * b:FT + 4096 + D * (b + 1)] for b in range(2)]
        qsb = W[:, FT + 6144:FT + 7168]
        val = W[:, FT + 7168:FT + 7424].rearrange("p (g k) -> p g k", k=TOPK)
        ind = W[:, FT + 7424:FT + 7680].bitcast(U32).rearrange("p (g k) -> p g k", k=TOPK)
        indf = W[:, FT + 7680:FT + 7936].rearrange("p (g k) -> p g k", k=TOPK)
        best = W[:, FT + 7936:FT + 8064].rearrange("p (h k) -> p h k", k=TOPK)
        pos = W[:, FT + 8064:FT + 8192].bitcast(U32).rearrange("p (h k) -> p h k", k=TOPK)
        rest = W[:, FT + 8192:FT + 8448]
        pick = W[:, FT + 8448:FT + 8704].rearrange("p (x k) -> p x k", x=2)
        diag = W[:, FT + 8704:FT + 9728].rearrange("p (j n) -> p j n", j=SLOTS)
        expert = [W[:, FT + 9728 + 128 * b:FT + 9856 + 128 * b].bitcast(U32) for b in range(2)]
        gate = [lat_r[:, 128 * b:128 * b + 128] for b in range(2)]
        soft = lat_r[:, 256:384]
        qTp = qTb
        skT = qn_r[:, 0:D].rearrange("p (h k) -> p h k", h=PH)
        slot = [S[:, 2 * D * b:2 * D * (b + 1)] for b in range(SLOTS)]
        score_bank = [0, 1, 4, 5]
        Y = P[:, 6:8, :]

        modTv = modT[:, :].rearrange("p (s j c) -> p s j c", s=2, j=MODS)
        gainv = gain[:, :].rearrange("p (s n c) -> p s n c", s=2, n=5)
        normv = normw[:, :].rearrange("p (n c) -> p n c", n=5)
        Gv = G[:, :].rearrange("p (s n) -> p s n", s=2)
        SHIFT = {"mix0": 0, "ffn0": 3, "mix1": 6, "ffn1": 9, "kv": 12}
        SCALE = {k: v + 1 for k, v in SHIFT.items()}
        GATE = {"mix0": 2, "ffn0": 5, "mix1": 8, "ffn1": 11}
        NORM = {"mix0": 0, "mix1": 1, "ffn0": 2, "ffn1": 3, "kv": 4}
        order = ([("mix0", t) for t in range(TILES)] + [("ffn0", t) for t in range(TILES)]
                 + [("kv", t) for t in range(TILES)] + [("mix1", t) for t in range(TILES)]
                 + [("ffn1", t) for t in range(TILES)])
        norm_at = {x: i for i, x in enumerate(order)}

        KEYS_A = [("new", t) for t in range(PT)] + [("past", 0), ("past", 1), ("new", PT)]
        key_at = {x: i for i, x in enumerate(KEYS_A)}

        mod_dram = nc.dram_tensor("mod_scratch", (2, MODS, D), F32).ap()

        def unit(layer, t):
            return layer * TILES + t

        def segments_of(t):
            return [(k, sum(SEGMENTS[t][:k]), n) for k, n in enumerate(SEGMENTS[t])]

        def first_step(layer, t):
            return layer * sum(STEPS) + sum(STEPS[:t])

        def second_start(t):
            return FIRST[t] * STEPS[t] // PH

        def keys_of(t):
            return 128 * (t + 1) if t < PT else PAST + DEC

        def blocks_of(t):
            n = keys_of(t)
            return [min(128, n - s) for s in range(0, n, 128)]

        def wait_alone(eng, name, value, passed):
            eng.wait_ge(sem(name), value)
            eng.sem_inc(sem(passed), 1)

        class Chain:

            def __init__(self, eng, name):
                self.eng, self.sem, self.n = eng, sem(name), 0

            def __call__(self, ins):
                self.n += 1
                ins.then_inc(self.sem, 1)
                self.eng.wait_ge(self.sem, self.n)

        block = ctx.enter_context(nc.Block())

        @block.sync
        def _(sp):
            def load(dst, src, name, **kw):
                sp.dma_start(dst, src, **kw).then_inc(sem(name), 16)

            load(cT[:, 0:2 * C].rearrange("p (s c) -> p s c", s=2), a["c"].rearrange("s (p c) -> p s c", c=C), "c_loaded")
            load(ada_bias, a["ada_b"].partition_broadcast(2), "bias_loaded")
            with sp.Fori(0, ADA_BLOCKS // 4) as r:
                for b in range(4):
                    sp.wait_ge(sem("ada_freed"), r * 4 + b + 1)
                    sp.dma_start(ada_w[b], a["ada_w"][bass.ds(r * 4 + b, 1), :, :].rearrange("a p (c n) -> (a p) c n", c=C)).then_inc(sem(f"ada_w{b}_loaded"), 16)
            load(ident[:, :], a["ident"], "const_loaded")
            load(iota[:, :], a["iota"], "const_loaded")
            load(rope[:, :], a["rope"], "const_loaded")
            load(masks[:, :], a["masks"], "const_loaded")
            load(normv, a["norms"].rearrange("n (p c) -> p n c", c=C), "const_loaded")
            load(rows_r[:, :], a["lora"].partition_broadcast(128), "const_loaded")
            load(qkw[:, :], a["qkw"].partition_broadcast(128), "const_loaded")
            for t in range(TILES):
                src = a["xp"][t * 128:(t + 1) * 128, :] if t < PT else a["xs"]
                load(xt[t][0:ROWS[t], :], src, "x_loaded")
            sp.wait_ge(sem("ada_freed"), ADA_BLOCKS + 2)
            load(w_in, a["w_in"].rearrange("(p c) n -> p c n", c=C), "w_in_loaded")
            sp.wait_ge(sem("mods_summed"), ADA_BLOCKS + 4)
            load(mod_dram.rearrange("s j n -> s (j n)"), ada_bias, "mods_stored")
            sp.wait_ge(sem("mods_stored"), 16)
            for s in range(2):
                load(modTv[:, s, :, :], mod_dram[s].rearrange("j (p c) -> p j c", c=C), "modT_loaded")
            load(w_uq, a["w_uq"].rearrange("(c p) n -> p c n", c=3), "w_uq_loaded")
            load(w_ukv, a["w_ukv"].rearrange("(c p) n -> p c n", c=2), "w_ukv_loaded")
            for s in range(2):
                load(Gv[:, s, :], mod_dram[s, GATE["mix0"], :].partition_broadcast(128), "gate_rows_loaded")
            load(w_oA, a["w_oA"].rearrange("(c p) n -> p c n", c=C), "w_oA_loaded")
            for t in range(TILES):
                if t == PT:
                    for k in range(2):
                        if k == 0:
                            sp.wait_ge(sem("lat_stored"), 32 * PT)
                            sp.wait_ge(sem("keys_multiplied"), PT)
                            sp.wait_ge(sem("q_multiplied"), PT)
                        sp.wait_ge(sem("keys_normed"), key_at["past", k])
                        sp.wait_ge(sem("keys_multiplied"), key_at["past", k])
                        load(latT[:, 3:5, :], a["past_ckvT"].rearrange("(c p) n -> p c n", c=2)[:, :, k * 128:(k + 1) * 128], "past_lat_loaded")
                        load(lat[:, 640:672], a["past_kr"][k * 128:(k + 1) * 128, :], "past_lat_loaded")
                r = ROWS[t]
                sp.wait_ge(sem("latents_normed"), t + 1)
                ckv, kr = (o["ckv_p"][t * 128:(t + 1) * 128, :], o["kr_p"][t * 128:(t + 1) * 128, :]) if t < PT else (o["ckv_s"], o["kr_s"])
                load(ckv, lat[0:r, Q_LORA:Q_LORA + KV_LORA], "lat_stored")
                load(kr, lat[0:r, 640:672], "lat_stored")
            for layer in range(2):
                sp.wait_ge(sem("q_multiplied"), unit(layer, TILES - 1) + 1)
                load(w_pq, a["p_w_q"][layer].rearrange("(p c) n -> p c n", c=C), "w_pq_loaded")
                sp.wait_ge(sem("mixed"), unit(layer, TILES - 1) + 1)
                for s in range(2):
                    load(Gv[:, s, :], mod_dram[s, GATE[f"ffn{layer}"], :].partition_broadcast(128), "gate_rows_loaded")
                load(skT, a["skT"][layer], "skT_loaded")
                if layer == 1:
                    break
                sp.wait_ge(sem("pq_multiplied"), 2 * TILES)
                load(w_k, a["w_kv"][:, 0:D].rearrange("(p c) n -> p c n", c=C), "w_k_loaded")
                load(rows_r[:, 0:2 * BD], a["bqk"].partition_broadcast(128), "bqk_loaded")
                sp.wait_ge(sem("experts_added"), unit(0, TILES - 1) + 1)
                load(w_v, a["w_kv"][:, D:2 * D].rearrange("(p c) n -> p c n", c=C), "w_v_loaded")
                for s in range(2):
                    load(Gv[:, s, :], mod_dram[s, GATE["mix1"], :].partition_broadcast(128), "gate_rows_loaded")
                load(KTs[:, :, 0:PAST], a["past_kT"].rearrange("(c p) n -> p c n", c=C), "past_kv_loaded")
                load(Vs[:, 0:2, :], a["past_v"].rearrange("(t p) n -> p t n", p=128), "past_kv_loaded")
                load(o["bk_s"][0:PAST - DEC, :], a["past_k"][DEC:PAST, :], "kept_past_stored")
                load(o["bv_s"][0:PAST - DEC, :], a["past_v"][DEC:PAST, :], "kept_past_stored")
                for t in range(TILES):
                    r = ROWS[t]
                    sp.wait_ge(sem("bk_normed"), t + 1)
                    dk, dv = (o["bk_p"][t * 128:(t + 1) * 128, :], o["bv_p"][t * 128:(t + 1) * 128, :]) if t < PT else (o["bk_s"][PAST - DEC:, :], o["bv_s"][PAST - DEC:, :])
                    load(dk, kn_r[0:r, 0:D], "bk_stored")
                    sp.wait_ge(sem("bv_copied"), t + 1)
                    load(dv, (Vp[:, t, :] if t < PT else Vs[:, 2, :])[0:r, :], "bv_stored")
                sp.wait_ge(sem("k_multiplied"), TILES)
                load(w_q, a["w_q"].rearrange("(p c) n -> p c n", c=C), "w_q_loaded")
                sp.wait_ge(sem("kv_multiplied"), TILES)
                load(w_oB, a["w_oB"].rearrange("(c p) n -> p c n", c=C), "w_oB_loaded")
                for n in range(TILES * HEADS):
                    if n >= 2:
                        sp.wait_ge(sem("max_ready"), TILES * HEADS + n - 1)
                    load(strips[n % 2], a["bias_strips"][n % HEADS], f"strip{n % 2}_loaded")
            for t in range(TILES):
                sp.wait_ge(sem("experts_added"), unit(1, t) + 1)
                load(o["y_p"][t * 128:(t + 1) * 128, :] if t < PT else o["y_s"], xt[t][0:ROWS[t], :], "y_stored")
            sp.wait_ge(sem("y_stored"), 16 * TILES)
            sp.wait_ge(sem("bk_stored"), 16 * TILES)
            sp.wait_ge(sem("bv_stored"), 16 * TILES)
            sp.wait_ge(sem("kept_past_stored"), 32)
            sp.wait_ge(sem("lat_stored"), 32 * TILES)

        @block.tensor
        def _(pe):
            nc_t = pe

            def products(out, lhs, rhs, n, chunks, r, first=0):
                for j in range(0, n, 512):
                    m = min(512, n - j)
                    for c in range(chunks):
                        ins = nc_t.matmul(out(j, m), lhs(c), rhs(c, j, m), start=(c == 0), stop=(c == chunks - 1))
                return ins

            def turn_norm(kind, t):
                r = ROWS[t]
                pe.wait_ge(sem("xn_ready"), norm_at[kind, t] + 1)
                for c in range(C):
                    ins = nc_t.transpose(P[:, 6 + c // 4, (c % 4) * 128:(c % 4) * 128 + r] if kind in ("kv", "mix1")
                                         else P[:, c // 4, (c % 4) * 128:(c % 4) * 128 + r],
                                         xn[0:r, c:D:C], ident[0:r, 0:r])
                ins.then_inc(sem("xn_turned"), 1)

            def attention(layer, t):
                r, nk, bl = ROWS[t], keys_of(t), blocks_of(t)
                n0 = unit(layer, t) * HEADS

                def scores(h):
                    n = n0 + h
                    if n >= 2:
                        pe.wait_ge(sem("probs_ready"), n - 1)
                    if layer == 0:
                        lhs, rhs = qT[0:QK, h, 0:r], KTa[0:QK, h, 0:nk]
                    else:
                        p0 = 64 * (h % 2)
                        lhs = qTb[p0:p0 + 64, h // 2, 0:r]
                        rhs = (KTp if t < PT else KTs)[p0:p0 + 64, h // 2, 0:nk]
                    bank = P[0:r, n % 2, 0:nk]
                    masked = layer == 0 and t < PT
                    ins = nc_t.matmul(bank, lhs, rhs, start=True, stop=not masked, skip_group_check=True)
                    if masked:
                        ins = nc_t.matmul(P[0:r, n % 2, nk - CHUNK:nk], masks[:, 0:128], masks[:, 128:128 + CHUNK],
                                          start=False, stop=True, skip_group_check=True)
                    ins.then_inc(sem("scores_ready"), 1)

                def turn(h):
                    n = n0 + h
                    pe.wait_ge(sem("turner_ready"), n + 1)
                    if n >= 2:
                        pe.wait_ge(sem("probs_copied"), n - 1)
                    for b, k in enumerate(bl):
                        ins = nc_t.matmul(P[0:k, 2 + n % 2, b * 128:b * 128 + r], probs[n % 2][0:r, b * 128:b * 128 + k],
                                          turner[n % 2][0:r, 0:r], start=True, stop=True, skip_group_check=True)
                    ins.then_inc(sem("probs_turned"), 1)

                def values(h):
                    n = n0 + h
                    pe.wait_ge(sem("probs_copied"), n + 1)
                    V = Va if layer == 0 else (Vp if t < PT else Vs)
                    p0, c = 64 * (h % 2), h // 2
                    for b, k in enumerate(bl):
                        ins = nc_t.matmul(P[p0:p0 + 64, 4 + c // 4, (c % 4) * 128:(c % 4) * 128 + r], V[0:k, b, h * 64:h * 64 + 64],
                                          probT[n % 2][0:k, b, 0:r], start=(b == 0), stop=(b == len(bl) - 1), skip_group_check=True)
                    ins.then_inc(sem("values_summed"), 1)

                for h in range(HEADS + 2):
                    if layer == 1 and t + 1 < TILES and h == AT_TURN:
                        if t:
                            pe.wait_ge(sem("mixed"), unit(1, t))
                        turn_norm("mix1", t + 1)
                    if h < HEADS:
                        scores(h)
                    if 1 <= h <= HEADS:
                        turn(h - 1)
                    if h >= 2:
                        values(h - 2)

            def out_product(layer, t):
                r, u = ROWS[t], unit(layer, t)
                w = w_oA if layer == 0 else w_oB
                pe.wait_ge(sem("heads_copied"), u + 1)
                pe.wait_ge(sem("w_oA_loaded" if layer == 0 else "w_oB_loaded"), 16)
                for b in range(2):
                    for c in range(C):
                        ins = nc_t.matmul(P[0:r, 6 + b, :], oT[:, c, 0:r], w[:, c, 512 * b:512 * b + 512], start=(c == 0), stop=(c == C - 1))
                    if b == 0 and layer == 0 and t + 1 < PT:
                        turn_norm("mix0", t + 1)
                ins.then_inc(sem("out_multiplied"), 1)

            pe.sem_inc(sem("ada_freed"), 4)
            pe.wait_ge(sem("c_ready"), 1)
            with pe.Fori(0, ADA_BLOCKS // 4) as g:
                for b in range(4):
                    pe.wait_ge(sem("mods_summed"), g * 4 + b + 1)
                    pe.wait_ge(sem(f"ada_w{b}_loaded"), (g + 1) * 16)
                    for c in range(C):
                        ins = nc_t.matmul(P[0:2, b, :], csT[:, c, :], ada_w[b][:, c, :], start=(c == 0), stop=(c == C - 1))
                    ins.then_inc(sem("ada_freed"), 1)

            def keys_A(kind, k):
                n = key_at[kind, k]
                r = ROWS[k] if kind == "new" else 128
                if kind == "past":
                    pe.wait_ge(sem("past_lat_loaded"), 32 * (k + 1))
                    pe.wait_ge(sem("keysT_copied"), n)
                    pe.wait_ge(sem("mixed"), PT)
                else:
                    pe.wait_ge(sem("w_ukv_loaded"), 16)
                if n:
                    pe.wait_ge(sem("v_copied"), n)
                ins = products(lambda j, m: P[0:r, 4 + j // 512, 0:m], lambda c: latT[:, 3 + c, 0:r], lambda c, j, m: w_ukv[:, c, j:j + m], 2 * D, 2, r)
                ins.then_inc(sem("keys_multiplied"), 1)

            def turn_keys_A(kind, k):
                n = key_at[kind, k]
                r = ROWS[k] if kind == "new" else 128
                pe.wait_ge(sem("keys_normed"), n + 1)
                pe.wait_ge(sem("v_copied"), n + 1)
                kn = kn_r[:, :].rearrange("p (h e) -> p h e", h=HEADS)
                for h in range(HEADS):
                    ins = nc_t.transpose(P[0:QK, 4 + h // 4, (h % 4) * 128:(h % 4) * 128 + r], kn[0:r, h, :], ident[0:r, 0:r])
                ins.then_inc(sem("keys_turned"), 1)

            pe.wait_ge(sem("const_loaded"), 16 * 7)
            for t in range(TILES):
                r = ROWS[t]
                if t == PT:
                    for k in range(2):
                        keys_A("past", k)
                        turn_keys_A("past", k)
                    pe.wait_ge(sem("keysT_copied"), PT + 2)
                if t in (0, PT):
                    turn_norm("mix0", t)
                if t:
                    pe.wait_ge(sem("mixed"), t)
                pe.wait_ge(sem("hT_ready"), norm_at["mix0", t] + 1)
                pe.wait_ge(sem("w_in_loaded"), 16)
                for lo, hi, bank in ((0, Q_LORA, 4), (Q_LORA, LAT, 5)):
                    for c in range(C):
                        ins = nc_t.matmul(P[0:r, bank, 0:hi - lo], hT[:, c, 0:r], w_in[:, c, lo:hi], start=(c == 0), stop=(c == C - 1))
                ins.then_inc(sem("latents_multiplied"), 1)
                pe.wait_ge(sem("latents_normed"), t + 1)
                for c in range(5):
                    ins = nc_t.transpose(P[:, 6 + (c >= 3), (c % 3) * 128:(c % 3) * 128 + r], lat[0:r, c * 128:(c + 1) * 128], ident[0:r, 0:r])
                ins.then_inc(sem("latents_turned"), 1)
                pe.wait_ge(sem("latents_copied"), t + 1)
                keys_A("new", t)
                pe.wait_ge(sem("w_uq_loaded"), 16)
                ins = products(lambda j, m: P[0:r, j // 512, 0:m], lambda c: latT[:, c, 0:r], lambda c, j, m: w_uq[:, c, j:j + m], HEADS * QK, 3, r)
                ins.then_inc(sem("q_multiplied"), 1)
                turn_keys_A("new", t)
                pe.wait_ge(sem("q_normed"), t + 1)
                qn = qn_r[:, :].rearrange("p (h e) -> p h e", h=HEADS)
                for h in range(HEADS):
                    ins = nc_t.transpose(P[0:QK, h // 4, (h % 4) * 128:(h % 4) * 128 + r], qn[0:r, h, :], ident[0:r, 0:r])
                ins.then_inc(sem("q_turned"), 1)
                pe.wait_ge(sem("qT_copied"), t + 1)
                pe.wait_ge(sem("keysT_copied"), key_at["new", t] + 1)
                attention(0, t)
                out_product(0, t)

            def select(layer, t, part):
                r, u = 128, unit(layer, t)
                if part in (1, 2):
                    b = part - 1
                    pe.wait_ge(sem("w_pq_loaded"), 16 * (layer + 1))
                    for c in range(C):
                        ins = nc_t.matmul(P[0:r, b, :], hT[:, c, 0:r], w_pq[:, c, 512 * b:512 * b + 512], start=(c == 0), stop=(c == C - 1))
                    ins.then_inc(sem("pq_multiplied"), 1)
                    return
                if part == 3:
                    pe.wait_ge(sem("pq_copied"), u + 1)
                    pe.wait_ge(sem("h_row_ready"), u + 1)
                    for c in range(C):
                        ins = nc_t.transpose(P[:, 2 + c // 4, (c % 4) * 128:(c % 4) * 128 + r], qsb[0:r, c * 128:(c + 1) * 128], ident[0:r, 0:r])
                    ins.then_inc(sem("pq_turned"), 1)
                    pe.wait_ge(sem("pqT_copied"), u + 1)
                    pe.wait_ge(sem("skT_loaded"), 16 * (layer + 1))
                    for g in range(2 * PH):
                        h, half = g // 2, g % 2
                        ins = nc_t.matmul(P[0:r, score_bank[2 * (h // 4) + g % 2], (h % 4) * 128:(h % 4) * 128 + 128],
                                          qTp[64 * half:64 * half + 64, h, 0:r], skT[64 * half:64 * half + 64, h, :], start=True, stop=True,
                                          skip_group_check=True)
                    ins.then_inc(sem("key_scores_ready"), 1)
                    return
                turn_norm(f"ffn{layer}", t)
                pe.wait_ge(sem("hT_ready"), norm_at[f"ffn{layer}", t] + 1)
                for c in range(C):
                    ins = nc_t.transpose(P[0:r, 2 + c // 4, (c % 4) * 128:(c % 4) * 128 + 128], hT[:, c, 0:r], ident[:, :])
                ins.then_inc(sem("h_turned_back"), 1)

            def experts(layer, t):
                r, u = ROWS[t], unit(layer, t)
                if u:
                    pe.wait_ge(sem("experts_added"), u)
                for b in range(2):
                    nc_t.matmul(Y[0:r, b, :], ident[:, 0:r], zero[:, 0:1].to_broadcast([128, 512]), start=True, stop=False, skip_group_check=True)
                for seg, start, steps in segments_of(t):
                    base = first_step(layer, t) + start
                    with pe.Fori(0, steps) as i:
                        for q in range(GROUPS):
                            wait_alone(pe, "weights_spread", i * GROUPS + (GROUPS * base + q + 1), "pe_passed")
                            for j in range(GROUP):
                                for b in range(2):
                                    ins = nc_t.matmul(Y[0:r, b, :], diag[:, GROUP * q + j, 0:r], slot[GROUP * q + j][:, D + 512 * b:D + 512 * b + 512],
                                                      start=False, stop=False, skip_group_check=True)
                            ins.then_inc(sem("slots_free"), 1)
                    if SELECT_AT <= seg < SELECT_AT + 4 and t + 1 < TILES:
                        select(layer, t + 1, seg - SELECT_AT)
                for b in range(2):
                    ins = nc_t.matmul(Y[0:r, b, :], ident[:, 0:r], zero[:, 0:1].to_broadcast([128, 512]), start=False, stop=True, skip_group_check=True)
                ins.then_inc(sem("experts_summed"), 1)

            pe.sem_inc(sem("slots_free"), GROUPS)
            for part in range(4):
                select(0, 0, part)
            for t in range(TILES):
                experts(0, t)

            turn_norm("kv", 0)
            for t in range(TILES):
                r = ROWS[t]
                h = hT_odd if t % 2 else hT
                pe.wait_ge(sem("hT_ready"), norm_at["kv", t] + 1)
                pe.wait_ge(sem("w_k_loaded"), 16)
                ins = products(lambda j, m: P[0:r, j // 512, 0:m], lambda c: h[:, c, 0:r], lambda c, j, m: w_k[:, c, j:j + m], D, C, r)
                ins.then_inc(sem("k_multiplied"), 1)
                if t + 1 < TILES:
                    turn_norm("kv", t + 1)
                pe.wait_ge(sem("w_v_loaded"), 16)
                if t:
                    pe.wait_ge(sem("bv_copied"), t)
                ins = products(lambda j, m: P[0:r, 2 + j // 512, 0:m], lambda c: h[:, c, 0:r], lambda c, j, m: w_v[:, c, j:j + m], D, C, r)
                ins.then_inc(sem("kv_multiplied"), 1)
                pe.wait_ge(sem("bk_normed"), t + 1)
                if t:
                    pe.wait_ge(sem("bkT_copied"), t)
                for c in range(C):
                    ins = nc_t.transpose(P[:, 4 + c // 4, (c % 4) * 128:(c % 4) * 128 + r], kn_r[0:r, c * 128:(c + 1) * 128], ident[0:r, 0:r])
                ins.then_inc(sem("bk_turned"), 1)
            def q_product_B(t):
                r = ROWS[t]
                pe.wait_ge(sem("hT_ready"), norm_at["mix1", t] + 1)
                pe.wait_ge(sem("w_q_loaded"), 16)
                pe.wait_ge(sem("bv_copied"), TILES)
                ins = products(lambda j, m: P[0:r, j // 512, 0:m], lambda c: hT[:, c, 0:r], lambda c, j, m: w_q[:, c, j:j + m], D, C, r)
                ins.then_inc(sem("q_multiplied"), 1)

            turn_norm("mix1", 0)
            q_product_B(0)
            for t in range(TILES):
                r, u = ROWS[t], unit(1, t)
                pe.wait_ge(sem("q_normed"), u + 1)
                pe.wait_ge(sem("bkT_copied"), TILES)
                for c in range(C):
                    ins = nc_t.transpose(P[:, 2 + c // 4, (c % 4) * 128:(c % 4) * 128 + r], qn_r[0:r, c * 128:(c + 1) * 128], ident[0:r, 0:r])
                ins.then_inc(sem("q_turned"), 1)
                pe.wait_ge(sem("qT_copied"), u + 1)
                if t == PT:
                    pe.wait_ge(sem("past_kv_loaded"), 32)
                attention(1, t)
                if t + 1 < TILES:
                    q_product_B(t + 1)
                out_product(1, t)
            for part in range(4):
                select(1, 0, part)
            for t in range(TILES):
                experts(1, t)

        @block.scalar
        def _(act):
            step = Chain(act, "act_steps")

            def squares(kind, t):
                r = ROWS[t]
                i = norm_at[kind, t]
                act.wait_ge(sem("x_loaded"), 16 * TILES)
                if i:
                    act.wait_ge(sem("xn_turned"), i)
                done, count = {"mix0": ("mixed", PT if t == PT else 0), "ffn0": ("mixed", TILES), "kv": ("experts_added", t + 1),
                               "mix1": ("experts_added", TILES), "ffn1": ("mixed", 2 * TILES)}[kind]
                if count:
                    act.wait_ge(sem(done), count)
                step(act.activation(xn[0:r, :], xt[t][0:r, :], ACT.Square, accum_out=stat[0:r, 0:1]))
                act.activation(stat[0:r, 1:2], stat[0:r, 0:1], ACT.Sqrt, scale=1.0 / D, bias=eps[0:r, :]).then_inc(sem("rms_ready"), 1)

            def attention(layer, t):
                r, nk = ROWS[t], keys_of(t)
                for h in range(HEADS):
                    if layer == 1 and t + 1 < TILES and h == AT_SQUARES:
                        squares("mix1", t + 1)
                    n = unit(layer, t) * HEADS + h
                    act.wait_ge(sem("max_ready"), n + 1)
                    if n >= 2:
                        act.wait_ge(sem("probs_turned"), n - 1)
                    src, sign = (P[0:r, n % 2, 0:nk], 1.0) if layer == 0 else (biased[n % 2][0:r, 0:nk], -1.0)
                    act.activation(probs[n % 2][0:r, 0:nk], src, ACT.Exp, scale=sign, bias=stat[0:r, 16 + n % 2:17 + n % 2],
                                   accum_out=row_sum[0:r, h:h + 1]).then_inc(sem("probs_ready"), 1)

            row_sum = stat[:, 32:48]

            act.wait_ge(sem("c_loaded"), 16)
            act.activation(cT[:, 2 * C:4 * C], cT[:, 0:2 * C], ACT.Exp, scale=-1.0).then_inc(sem("c_exp"), 1)
            act.wait_ge(sem("eps_ready"), 1)

            def copy_heads(u, r):
                act.wait_ge(sem("values_summed"), HEADS * (u + 1))
                for b in range(2):
                    ins = act.copy(oT[:, 4 * b:4 * b + 4, 0:r], P[:, 4 + b, :].rearrange("p (c n) -> p c n", c=4)[:, :, 0:r])
                ins.then_inc(sem("heads_copied"), 1)

            def keys_A(kind, k):
                n = key_at[kind, k]
                r = ROWS[k] if kind == "new" else 128
                act.wait_ge(sem("keys_multiplied"), n + 1)
                if n:
                    act.wait_ge(sem("keys_squares_summed"), n)
                if kind == "past" or k:
                    act.wait_ge(sem("q_normed"), k if kind == "new" else PT)
                act.activation(T1[0:r, 0:512], P[0:r, 4, :], ACT.Square)
                act.activation(T1[0:r, 512:1024], P[0:r, 5, :], ACT.Square).then_inc(sem("keys_squared"), 1)
                vt = (k if k < PT else 2) if kind == "new" else k
                if kind == "past" and k == 0:
                    act.wait_ge(sem("values_summed"), HEADS * PT)
                act.copy(Va[0:r, vt, 0:512], P[0:r, 6, :])
                act.copy(Va[0:r, vt, 512:1024], P[0:r, 7, :]).then_inc(sem("v_copied"), 1)
                act.wait_ge(sem("keys_squares_summed"), n + 1)
                act.activation(stat[0:r, 48:64], stat[0:r, 32:48], ACT.Sqrt, scale=1.0 / QK, bias=eps[0:r, :]).then_inc(sem("keys_rms"), 1)

            for t in range(TILES):
                r = ROWS[t]
                if t == PT:
                    keys_A("past", 0)
                    keys_A("past", 1)
                if t in (0, PT):
                    squares("mix0", t)
                act.wait_ge(sem("latents_multiplied"), t + 1)
                act.activation(T1[0:r, 0:Q_LORA], P[0:r, 4, 0:Q_LORA], ACT.Square, accum_out=stat[0:r, 2:3])
                step(act.activation(T1[0:r, 512:512 + KV_LORA], P[0:r, 5, 0:KV_LORA], ACT.Square, accum_out=stat[0:r, 3:4]))
                act.activation(stat[0:r, 4:5], stat[0:r, 2:3], ACT.Sqrt, scale=1.0 / Q_LORA, bias=eps[0:r, :])
                act.activation(stat[0:r, 5:6], stat[0:r, 3:4], ACT.Sqrt, scale=1.0 / KV_LORA, bias=eps[0:r, :]).then_inc(sem("latents_rms"), 1)
                act.wait_ge(sem("latents_turned"), t + 1)
                act.copy(latT[:, 0:3, 0:r], P[:, 6, 0:384].rearrange("p (c n) -> p c n", c=3)[:, :, 0:r])
                act.copy(latT[:, 3:5, 0:r], P[:, 7, 0:256].rearrange("p (c n) -> p c n", c=2)[:, :, 0:r]).then_inc(sem("latents_copied"), 1)
                keys_A("new", t)
                act.wait_ge(sem("q_multiplied"), t + 1)
                for b in range(3):
                    ins = act.activation(qT_r[0:r, 512 * b:512 * (b + 1)], P[0:r, b, :], ACT.Square)
                ins.then_inc(sem("q_squared"), 1)
                act.wait_ge(sem("q_squares_summed"), t + 1)
                act.activation(stat[0:r, 48:64], stat[0:r, 32:48], ACT.Sqrt, scale=1.0 / QK, bias=eps[0:r, :]).then_inc(sem("q_rms"), 1)
                act.wait_ge(sem("q_turned"), t + 1)
                for b in range(4):
                    ins = act.copy(qT[0:QK, 4 * b:4 * b + 4, 0:r], P[0:QK, b, :].rearrange("p (c n) -> p c n", c=4)[:, :, 0:r])
                ins.then_inc(sem("qT_copied"), 1)
                act.wait_ge(sem("keys_normed"), key_at["new", t] + 1)
                attention(0, t)
                copy_heads(t, r)
                if t + 1 < PT:
                    squares("mix0", t + 1)

            def select(layer, t, part):
                r, u = 128, unit(layer, t)
                if part == 0:
                    squares(f"ffn{layer}", t)
                    act.wait_ge(sem("h_turned_back"), u + 1)
                    for b in range(2):
                        ins = act.copy(hrow[u % 2][0:r, :].rearrange("n (p c) -> n c p", c=C)[:, 4 * b:4 * b + 4, :],
                                       P[0:r, 2 + b, :].rearrange("n (c p) -> n c p", c=4))
                    ins.then_inc(sem("h_row_ready"), 1)
                    return
                if part == 1:
                    return
                b = part - 2
                act.wait_ge(sem("pq_multiplied"), 2 * u + b + 1)
                ins = act.copy(qsb[0:r, 512 * b:512 * b + 512], P[0:r, b, :])
                if part == 2:
                    return
                ins.then_inc(sem("pq_copied"), 1)
                act.wait_ge(sem("pq_turned"), u + 1)
                for b in range(2):
                    ins = act.copy(qTp[:, 4 * b:4 * b + 4, 0:r], P[:, 2 + b, :].rearrange("p (c n) -> p c n", c=4)[:, :, 0:r])
                ins.then_inc(sem("pqT_copied"), 1)

            def choose_exp(layer, t, group):
                r, u = 128, unit(layer, t)
                act.wait_ge(sem("best_shifted"), 2 * u + group + 1)
                sf = soft[0:r, 0:FIRST[t] * TOPK] if group == 0 else soft[0:r, FIRST[t] * TOPK:]
                act.activation(sf, sf, ACT.Exp).then_inc(sem("best_exp"), 1)

            def experts(layer, t):
                r, u = 128, unit(layer, t)
                for seg, start, steps in segments_of(t):
                    base = first_step(layer, t) + start
                    with act.Fori(0, steps) as i:
                        for q in range(GROUPS):
                            act.wait_ge(sem("dots_ready"), i * GROUPS + (GROUPS * base + q + 1))
                            act.activation(dots[0:r, SLOTS + GROUP * q:SLOTS + GROUP * (q + 1)], dots[0:r, GROUP * q:GROUP * (q + 1)],
                                           ACT.Gelu_apprx_tanh).then_inc(sem("gelu_ready"), 1)
                    if seg == (3 if t < PT else 2):
                        choose_exp(layer, t, 1)
                    if t + 1 < TILES:
                        if SELECT_AT <= seg < SELECT_AT + 4:
                            select(layer, t + 1, seg - SELECT_AT)
                        if seg == 10:
                            choose_exp(layer, t + 1, 0)

            for part in range(4):
                select(0, 0, part)
            choose_exp(0, 0, 0)
            for t in range(TILES):
                experts(0, t)
            squares("kv", 0)
            for t in range(TILES):
                r = ROWS[t]
                if t + 1 < TILES:
                    squares("kv", t + 1)
                act.wait_ge(sem("k_multiplied"), t + 1)
                for b in range(2):
                    ins = act.activation(T1[0:r, 1024 + 512 * b:1536 + 512 * b], P[0:r, b, :], ACT.Square)
                ins.then_inc(sem("bk_squared"), 1)
                act.wait_ge(sem("bk_squares_summed"), t + 1)
                act.activation(stat[0:r, 48:64], stat[0:r, 32:48], ACT.Sqrt, scale=1.0 / BD, bias=eps[0:r, :]).then_inc(sem("bk_rms"), 1)
                act.wait_ge(sem("kv_multiplied"), t + 1)
                v = Vp[:, t, :] if t < PT else Vs[:, 2, :]
                for b in range(2):
                    ins = act.copy(v[0:r, 512 * b:512 * b + 512], P[0:r, 2 + b, :])
                ins.then_inc(sem("bv_copied"), 1)
            def q_squares_B(t):
                r, u = ROWS[t], unit(1, t)
                act.wait_ge(sem("q_multiplied"), u + 1)
                if t >= 2:
                    act.wait_ge(sem("mixed"), u - 1)
                for b in range(2):
                    ins = act.activation(T1[0:r, 1024 + 512 * b:1536 + 512 * b], P[0:r, b, :], ACT.Square)
                ins.then_inc(sem("q_squared"), 1)
                act.wait_ge(sem("q_squares_summed"), u + 1)
                act.activation(stat[0:r, 48:64], stat[0:r, 32:48], ACT.Sqrt, scale=1.0 / BD, bias=eps[0:r, :]).then_inc(sem("q_rms"), 1)

            squares("mix1", 0)
            q_squares_B(0)
            for t in range(TILES):
                r, u = ROWS[t], unit(1, t)
                act.wait_ge(sem("q_turned"), u + 1)
                for b in range(2):
                    ins = act.copy(qTb[:, 4 * b:4 * b + 4, 0:r], P[:, 2 + b, :].rearrange("p (c n) -> p c n", c=4)[:, :, 0:r])
                ins.then_inc(sem("qT_copied"), 1)
                attention(1, t)
                copy_heads(u, r)
                if t + 1 < TILES:
                    q_squares_B(t + 1)
            for part in range(4):
                select(1, 0, part)
            choose_exp(1, 0, 0)
            for t in range(TILES):
                experts(1, t)

        @block.vector
        def _(dve):
            step = Chain(dve, "dve_steps")
            row_sum = stat[:, 32:48]

            def bc(ap, shape):
                return ap.to_broadcast(shape)

            def normalise(kind, t):
                divide(kind, t)
                modulate(kind, t)

            def divide(kind, t):
                r, i = ROWS[t], norm_at[kind, t]
                dve.wait_ge(sem("rms_ready"), i + 1)
                step(dve.reciprocal(stat[0:r, 6:7], stat[0:r, 1:2]))
                dve.tensor_scalar(xn[0:r, :], xt[t][0:r, :], stat[0:r, 6:7], None, ALU.mult).then_inc(sem("xn_ready"), 1)

            def modulate(kind, t):
                r, s, i = ROWS[t], seq_of(t), norm_at[kind, t]
                dve.wait_ge(sem("xn_turned"), i + 1)
                b0 = 6 if kind in ("kv", "mix1") else 0
                dst = hT_odd if kind == "kv" and t % 2 else hT
                for c in range(C):
                    ins = dve.tensor_scalar(dst[:, c, 0:r], P[:, b0 + c // 4, (c % 4) * 128:(c % 4) * 128 + r],
                                            gainv[:, s, NORM[kind], c:c + 1], modTv[:, s, SHIFT[kind], c:c + 1], ALU.mult, ALU.add)
                if kind[:3] == "ffn" and t == PT:
                    step(ins)
                    ins = dve.tensor_copy(hT[:, :, DEC:2 * DEC], hT[:, :, 0:DEC])
                ins.then_inc(sem("hT_ready"), 1)

            def rotate(x, r, tile):
                x1, x2 = x[0:r, :, NOPE:NOPE + HALF], x[0:r, :, NOPE + HALF:QK]
                tab = rope[0:r, tile * ROPE:(tile + 1) * ROPE]
                cos, sin = (bc(tab[:, i * HALF:(i + 1) * HALF].unsqueeze(1), [r, HEADS, HALF]) for i in range(2))
                p = [T1[0:r, 1024 + 256 * i:1280 + 256 * i].rearrange("p (h e) -> p h e", h=HEADS) for i in range(4)]
                dve.tensor_tensor(p[0], x1, cos, ALU.mult)
                dve.tensor_tensor(p[1], x2, sin, ALU.mult)
                dve.tensor_tensor(p[2], x2, cos, ALU.mult)
                step(dve.tensor_tensor(p[3], x1, sin, ALU.mult))
                dve.tensor_tensor(x1, p[0], p[1], ALU.subtract)
                return dve.tensor_tensor(x2, p[2], p[3], ALU.add)

            def add_mixed(layer, t):
                r, u, s = ROWS[t], unit(layer, t), seq_of(t)
                dve.wait_ge(sem("out_multiplied"), u + 1)
                dve.wait_ge(sem("gate_rows_loaded"), 32 * (2 * layer + 1))
                step(dve.tensor_tensor(T1[0:r, D:2 * D].rearrange("p (b n) -> p b n", b=2), P[0:r, 6:8, :],
                                       Gv[0:r, s, :].rearrange("p (b n) -> p b n", b=2), ALU.mult))
                ins = dve.tensor_tensor(xt[t][0:r, :], xt[t][0:r, :], T1[0:r, D:2 * D], ALU.add)
                ins.then_inc(sem("mixed"), 1)
                dve.wait_ge(sem("mixed"), u + 1)

            def attention(layer, t):
                r, nk, bl = ROWS[t], keys_of(t), blocks_of(t)

                def largest(h):
                    n = unit(layer, t) * HEADS + h
                    dve.wait_ge(sem("scores_ready"), n + 1)
                    if n >= 2:
                        dve.wait_ge(sem("probs_ready"), n - 1)
                    peak = stat[0:r, 16 + n % 2:17 + n % 2]
                    if layer == 0:
                        dve.tensor_reduce(peak, P[0:r, n % 2, 0:nk], AX.X, ALU.max, negate=True).then_inc(sem("max_ready"), 1)
                        return
                    m = n - TILES * HEADS
                    off = STRIP - nk if t < PT else 128
                    dve.wait_ge(sem(f"strip{m % 2}_loaded"), 16 * (m // 2 + 1))
                    dve.tensor_tensor_reduce(biased[n % 2][0:r, 0:nk], P[0:r, n % 2, 0:nk], strips[m % 2][0:r, off:off + nk], -1.0, -LOWEST,
                                             ALU.add, ALU.min, peak).then_inc(sem("max_ready"), 1)

                def invert(h):
                    n = unit(layer, t) * HEADS + h
                    dve.wait_ge(sem("probs_ready"), n + 1)
                    if n >= 2:
                        dve.wait_ge(sem("probs_turned"), n - 1)
                    step(dve.reciprocal(stat[0:r, 18:19], row_sum[0:r, h:h + 1]))
                    dve.tensor_scalar(turner[n % 2][0:r, 0:r], ident[0:r, 0:r], stat[0:r, 18:19], None, ALU.mult)\
                       .then_inc(sem("turner_ready"), 1)

                def copy_probs(h):
                    n = unit(layer, t) * HEADS + h
                    dve.wait_ge(sem("probs_turned"), n + 1)
                    if n >= 2:
                        dve.wait_ge(sem("values_summed"), n - 1)
                    full = sum(k == 128 for k in bl)
                    src = P[:, 2 + n % 2, :].rearrange("p (b n) -> p b n", n=128)
                    ins = dve.tensor_copy(probT[n % 2][:, 0:full, 0:r], src[:, 0:full, 0:r])
                    if full < len(bl):
                        ins = dve.tensor_copy(probT[n % 2][0:bl[-1], full, 0:r], src[0:bl[-1], full, 0:r])
                    ins.then_inc(sem("probs_copied"), 1)

                for h in range(HEADS + 2):
                    if layer == 1 and t + 1 < TILES:
                        if h == AT_NORM:
                            divide("mix1", t + 1)
                        elif h == AT_GAIN:
                            modulate("mix1", t + 1)
                    if h >= 2:
                        copy_probs(h - 2)
                    if 1 <= h <= HEADS:
                        invert(h - 1)
                    if h < HEADS:
                        largest(h)

            dve.memset(zero[:, :], 0.0)
            dve.memset(eps[:, :], EPS).then_inc(sem("eps_ready"), 1)
            dve.wait_ge(sem("c_exp"), 1)
            step(dve.tensor_scalar(cT[:, 2 * C:4 * C], cT[:, 2 * C:4 * C], 1.0, None, ALU.add))
            step(dve.reciprocal(cT[:, 2 * C:4 * C], cT[:, 2 * C:4 * C]))
            dve.tensor_tensor(csT, cT[:, 0:2 * C].rearrange("p (s c) -> p c s", s=2),
                              cT[:, 2 * C:4 * C].rearrange("p (s c) -> p c s", s=2), ALU.mult).then_inc(sem("c_ready"), 1)
            dve.wait_ge(sem("bias_loaded"), 16)
            dve.sem_inc(sem("mods_summed"), 4)
            with dve.Fori(0, ADA_BLOCKS // 4) as g:
                for b in range(4):
                    dve.wait_ge(sem("ada_freed"), g * 4 + (b + 5))
                    row = ada_bias[:, bass.ds((g * 4 + b) * ADA_BLOCK, ADA_BLOCK)]
                    dve.tensor_tensor(row, P[0:2, b, :], row, ALU.add).then_inc(sem("mods_summed"), 1)
            dve.wait_ge(sem("modT_loaded"), 16 * 2)
            dve.wait_ge(sem("const_loaded"), 16 * 7)
            for kind in NORM:
                for s in range(2):
                    dve.scalar_tensor_tensor(gainv[:, s, NORM[kind], :], modTv[:, s, SCALE[kind], :], 1.0, normv[:, NORM[kind], :], ALU.add, ALU.mult)
            step(dve.tensor_scalar(qkw[:, 0:QK], qkw[:, 0:QK], float(QK) ** -0.5, None, ALU.mult))

            def keys_A(kind, k):
                n = key_at[kind, k]
                r = ROWS[k] if kind == "new" else 128
                kn = kn_r[:, :].rearrange("p (h e) -> p h e", h=HEADS)
                dve.wait_ge(sem("keys_squared"), n + 1)
                if kind == "past":
                    dve.wait_ge(sem("past_lat_loaded"), 32 * (k + 1))
                step(dve.tensor_tensor(T1[0:r, 1024:1024 + ROPE], lat[0:r, 640:672], lat[0:r, 640:672], ALU.mult))
                dve.tensor_reduce(stat[0:r, 7:8], T1[0:r, 1024:1024 + ROPE], AX.X, ALU.add)
                step(dve.tensor_reduce(stat[0:r, 32:48], T1[0:r, 0:D].rearrange("p (h e) -> p h e", h=HEADS), AX.X, ALU.add))
                dve.tensor_scalar(stat[0:r, 32:48], stat[0:r, 32:48], stat[0:r, 7:8], None, ALU.add).then_inc(sem("keys_squares_summed"), 1)
                dve.wait_ge(sem("keys_rms"), n + 1)
                step(dve.reciprocal(stat[0:r, 48:64], stat[0:r, 48:64]))
                if n:
                    dve.wait_ge(sem("keys_turned"), n)
                inv = stat[0:r, 48:64].unsqueeze(2)
                for b in range(2):
                    dve.tensor_tensor(kn[0:r, 8 * b:8 * b + 8, 0:NOPE], P[0:r, 4 + b, :].rearrange("p (h e) -> p h e", h=8),
                                      bc(inv[:, 8 * b:8 * b + 8, :], [r, 8, NOPE]), ALU.mult)
                step(dve.tensor_tensor(kn[0:r, :, NOPE:QK], bc(lat[0:r, 640:672].unsqueeze(1), [r, HEADS, ROPE]), bc(inv, [r, HEADS, ROPE]), ALU.mult))
                step(dve.tensor_tensor(kn[0:r, :, :], kn[0:r, :, :], bc(qkw[0:r, QK:2 * QK].unsqueeze(1), [r, HEADS, QK]), ALU.mult))
                tile = (k if k < PT else 2) if kind == "new" else k
                rotate(kn, r, tile).then_inc(sem("keys_normed"), 1)

            def copy_keys_A(kind, k):
                n = key_at[kind, k]
                r = ROWS[k] if kind == "new" else 128
                tile = (k if k < PT else 2) if kind == "new" else k
                dve.wait_ge(sem("keys_turned"), n + 1)
                for b in range(4):
                    ins = dve.tensor_copy(KTa[0:QK, 4 * b:4 * b + 4, tile * 128:tile * 128 + r],
                                          P[0:QK, 4 + b, :].rearrange("p (h n) -> p h n", h=4)[:, :, 0:r])
                ins.then_inc(sem("keysT_copied"), 1)

            for t in range(TILES):
                r = ROWS[t]
                if t == PT:
                    for k in range(2):
                        keys_A("past", k)
                        copy_keys_A("past", k)
                if t in (0, PT):
                    normalise("mix0", t)
                dve.wait_ge(sem("latents_rms"), t + 1)
                step(dve.reciprocal(stat[0:r, 4:6], stat[0:r, 4:6]))
                if t:
                    dve.wait_ge(sem("lat_stored"), 32 * t)
                if t == PT:
                    dve.wait_ge(sem("keys_normed"), PT + 2)
                dve.scalar_tensor_tensor(lat[0:r, 0:Q_LORA], P[0:r, 4, 0:Q_LORA], stat[0:r, 4:5], rows_r[0:r, 0:Q_LORA], ALU.mult, ALU.mult)
                dve.scalar_tensor_tensor(lat[0:r, Q_LORA:640], P[0:r, 5, 0:KV_LORA], stat[0:r, 5:6], rows_r[0:r, Q_LORA:640], ALU.mult, ALU.mult)
                dve.tensor_copy(lat[0:r, 640:672], P[0:r, 5, KV_LORA:KV_LORA + ROPE]).then_inc(sem("latents_normed"), 1)
                qn = qn_r[:, :].rearrange("p (h e) -> p h e", h=HEADS)
                keys_A("new", t)
                dve.wait_ge(sem("q_squared"), t + 1)
                dve.tensor_reduce(stat[0:r, 32:48], qT_r[0:r, 0:HEADS * QK].rearrange("p (h e) -> p h e", h=HEADS), AX.X, ALU.add).then_inc(sem("q_squares_summed"), 1)
                dve.wait_ge(sem("q_rms"), t + 1)
                step(dve.reciprocal(stat[0:r, 48:64], stat[0:r, 48:64]))
                step(dve.tensor_tensor(qn[0:r, :, :], P[0:r, 0:3, :].rearrange("p b n -> p (b n)").rearrange("p (h e) -> p h e", h=HEADS),
                                       bc(stat[0:r, 48:64].unsqueeze(2), [r, HEADS, QK]), ALU.mult))
                step(dve.tensor_tensor(qn[0:r, :, :], qn[0:r, :, :], bc(qkw[0:r, 0:QK].unsqueeze(1), [r, HEADS, QK]), ALU.mult))
                rotate(qn, r, t if t < PT else 2).then_inc(sem("q_normed"), 1)
                dve.wait_ge(sem("q_normed"), t + 1)
                copy_keys_A("new", t)
                attention(0, t)
                if t + 1 < PT:
                    normalise("mix0", t + 1)
                add_mixed(0, t)

            def top16(r, src, values, indices, length, spare):
                step(dve.max(values[:, 0:8], src))
                dve.max_index(indices[:, 0:8], values[:, 0:8], src)
                step(dve.match_replace(spare, values[:, 0:8], src, LOWEST))
                step(dve.max(values[:, 8:16], spare))
                step(dve.max_index(indices[:, 8:16], values[:, 8:16], spare))

            def choose_heads(layer, t, heads):
                r, u = 128, unit(layer, t)
                dve.wait_ge(sem("key_scores_ready"), u + 1)
                for h in heads:
                    for g in (2 * h, 2 * h + 1):
                        src = P[0:r, score_bank[2 * (h // 4) + g % 2], (h % 4) * 128:(h % 4) * 128 + 128]
                        top16(r, src, val[0:r, g, :], ind[0:r, g, :], NKEYS, rest[0:r, 0:NKEYS])
                    cd = cand[0:r, h * 256:(h + 1) * 256]
                    step(dve.tensor_tensor(cd.rearrange("p (a b) -> p a b", a=TOPK),
                                           bc(val[0:r, 2 * h, :].unsqueeze(2), [r, TOPK, TOPK]),
                                           bc(val[0:r, 2 * h + 1, :].unsqueeze(1), [r, TOPK, TOPK]), ALU.add))
                    top16(r, cd, best[0:r, h, :], pos[0:r, h, :], 256, rest[0:r, :])

            def decode(layer, t, group):
                r, u = 128, unit(layer, t)
                lo, hi = ((0, FIRST[t]), (FIRST[t], PH))[group]
                n, at = hi - lo, slice(lo * TOPK, hi * TOPK)
                sf = soft[0:r, at].rearrange("p (h k) -> p h k", h=n)
                dve.tensor_tensor(sf, best[0:r, lo:hi, :], bc(best[0:r, lo:hi, 0:1], [r, n, TOPK]), ALU.subtract).then_inc(sem("best_shifted"), 1)
                ch = cand[0:r, lo * 256:hi * 256].rearrange("p (g k j) -> p g k j", g=n, k=TOPK)
                ht = hot[0:r, lo * 256:hi * 256].rearrange("p (g k j) -> p g k j", g=n, k=TOPK)
                pk = pick[0:r, :, at].bitcast(U32)
                pf = pos[0:r, lo:hi, :].rearrange("p h k -> p (h k)")
                dve.tensor_scalar(pk[:, 0, :], pf, 4, None, ALU.logical_shift_right)
                step(dve.tensor_scalar(pk[:, 1, :], pf, 15, None, ALU.bitwise_and))
                dve.tensor_copy(pick[0:r, :, at], pk)
                step(dve.tensor_copy(indf[0:r, 2 * lo:2 * hi, :], ind[0:r, 2 * lo:2 * hi, :]))
                for x in range(2):
                    tab = indf[0:r, 2 * lo + x:2 * hi:2, :].unsqueeze(2)
                    step(dve.tensor_tensor(ch.rearrange("p g k j -> p (g k) j"),
                                           bc(iota[0:r, :].unsqueeze(1), [r, n * TOPK, TOPK]),
                                           bc(pick[0:r, x, at].unsqueeze(2), [r, n * TOPK, TOPK]), ALU.is_equal))
                    step(dve.tensor_tensor(ht, ch, bc(tab, [r, n, TOPK, TOPK]), ALU.mult))
                    step(dve.tensor_reduce(hsum[0:r, x, at], ht.rearrange("p g k j -> p (g k) j"), AX.X, ALU.add))
                parts = [(0, 128, 0, 1)] if t < PT else [(0, DEC, 0, 2), (DEC, 2 * DEC, 1, 2)]
                for p, e, off, every in parts:
                    dve.scalar_tensor_tensor(expert[u % 2][p:e, lo * TOPK // every:hi * TOPK // every],
                                             hsum[p:e, 0, lo * TOPK + off:hi * TOPK:every], float(NKEYS),
                                             hsum[p:e, 1, lo * TOPK + off:hi * TOPK:every], ALU.mult, ALU.add)
                dve.wait_ge(sem("best_exp"), 2 * u + group + 1)
                step(dve.tensor_reduce(stat[0:r, 24:24 + n], sf, AX.X, ALU.add))
                step(dve.reciprocal(stat[0:r, 24:24 + n], stat[0:r, 24:24 + n]))
                for p, e, off, every in parts:
                    ins = dve.tensor_tensor(gate[u % 2][p:e, lo * TOPK // every:hi * TOPK // every].rearrange("p (h k) -> p h k", h=n),
                                            soft[p:e, at].rearrange("p (h k) -> p h k", h=n)[:, :, off:TOPK:every],
                                            bc(stat[p:e, 24:24 + n].unsqueeze(2), [e - p, n, TOPK // every]), ALU.mult)
                ins.then_inc(sem("experts_chosen"), 1)
                dve.wait_ge(sem("experts_chosen"), 2 * u + group + 1)

            hsum = lat_r[:, 384:640].rearrange("p (x k) -> p x k", x=2)

            def experts(layer, t):
                r, u, s = ROWS[t], unit(layer, t), seq_of(t)
                pattern = ident if t < PT else both
                for seg, start, steps in segments_of(t):
                    base = first_step(layer, t) + start
                    with dve.Fori(0, steps) as i:
                        for q in range(GROUPS):
                            for b in range(GROUP * q, GROUP * (q + 1)):
                                dve.wait_ge(sem(f"rows{b}_gathered"), i * 16 + 16 * (base + 1))
                                ins = dve.tensor_tensor_reduce(slot[b][:, 0:D], slot[b][:, 0:D], hrow[u % 2][:, :], 1.0, 0.0,
                                                               ALU.mult, ALU.add, dots[:, b:b + 1])
                            ins.then_inc(sem("dots_ready"), 1)
                            nth = i * GROUPS + (GROUPS * base + q + 1)
                            dve.wait_ge(sem("gelu_ready"), nth)
                            wts = dots[:, 2 * SLOTS + GROUP * q:2 * SLOTS + GROUP * (q + 1)]
                            dve.tensor_tensor(wts, dots[:, SLOTS + GROUP * q:SLOTS + GROUP * (q + 1)],
                                              gate[u % 2][:, bass.ds(i * SLOTS + (start * SLOTS + GROUP * q), GROUP)],
                                              ALU.mult).then_inc(sem("weights_ready"), 1)
                            dve.wait_ge(sem("weights_ready"), nth)
                            dve.tensor_tensor(diag[:, GROUP * q:GROUP * (q + 1), 0:r], bc(pattern[:, 0:r].unsqueeze(1), [128, GROUP, r]),
                                              bc(wts.unsqueeze(2), [128, GROUP, r]), ALU.mult).then_inc(sem("weights_spread"), 1)
                    own = ((3, 4), (5, 6), (7,)) if t < PT else ((4, 5), (6, 7))
                    if seg < len(own):
                        choose_heads(layer, t, own[seg])
                    elif seg == len(own):
                        decode(layer, t, 1)
                    elif t + 1 < TILES:
                        if seg == SELECT_AT:
                            normalise(f"ffn{layer}", t + 1)
                        elif seg in (8, 9):
                            choose_heads(layer, t + 1, ((0, 1), range(2, FIRST[t + 1]))[seg - 8])
                        elif seg == 10:
                            decode(layer, t + 1, 0)
                dve.wait_ge(sem("experts_summed"), u + 1)
                if t == 0:
                    dve.wait_ge(sem("gate_rows_loaded"), 32 * (2 * layer + 2))
                step(dve.tensor_tensor(hot[0:r, 0:D].rearrange("p (b n) -> p b n", b=2), Y[0:r, :, :],
                                       Gv[0:r, s, :].rearrange("p (b n) -> p b n", b=2), ALU.mult))
                dve.tensor_tensor(xt[t][0:r, :], xt[t][0:r, :], hot[0:r, 0:D], ALU.add).then_inc(sem("experts_added"), 1)

            both = rows_r[:, 128:128 + DEC]

            def mixer(layer):
                if layer == 0:
                    step(dve.tensor_tensor(both, ident[:, 0:DEC], ident[:, DEC:2 * DEC], ALU.add))
                normalise(f"ffn{layer}", 0)
                choose_heads(layer, 0, range(FIRST[0]))
                decode(layer, 0, 0)
                for t in range(TILES):
                    experts(layer, t)
                    dve.wait_ge(sem("experts_added"), unit(layer, t) + 1)

            mixer(0)
            dve.wait_ge(sem("experts_added"), TILES)

            def head_norm(r, banks, dst, w, squares, summed, rms, n):
                dve.wait_ge(sem(squares), n + 1)
                dve.tensor_reduce(stat[0:r, 32:48], T1[0:r, D:2 * D].rearrange("p (h e) -> p h e", h=HEADS), AX.X, ALU.add).then_inc(sem(summed), 1)
                dve.wait_ge(sem(rms), n + 1)
                step(dve.reciprocal(stat[0:r, 48:64], stat[0:r, 48:64]))
                for b in range(2):
                    ins = dve.tensor_tensor(dst[0:r, 512 * b:512 * b + 512].rearrange("p (h e) -> p h e", h=8),
                                            P[0:r, banks + b, :].rearrange("p (h e) -> p h e", h=8),
                                            bc(stat[0:r, 48 + 8 * b:56 + 8 * b].unsqueeze(2), [r, 8, BD]), ALU.mult)
                step(ins)
                x = dst[0:r, 0:D].rearrange("p (h e) -> p h e", h=HEADS)
                return dve.tensor_tensor(x, x, bc(w[0:r, :].unsqueeze(1), [r, HEADS, BD]), ALU.mult)

            dve.wait_ge(sem("bqk_loaded"), 16)
            step(dve.tensor_scalar(rows_r[:, 0:BD], rows_r[:, 0:BD], float(BD) ** -0.5, None, ALU.mult))
            normalise("kv", 0)
            for t in range(TILES):
                r = ROWS[t]
                if t + 1 < TILES:
                    normalise("kv", t + 1)
                if t:
                    dve.wait_ge(sem("bk_stored"), 16 * t)
                head_norm(r, 0, kn_r, rows_r[:, BD:2 * BD], "bk_squared", "bk_squares_summed", "bk_rms", t).then_inc(sem("bk_normed"), 1)
                dve.wait_ge(sem("bk_turned"), t + 1)
                kt, at = (KTp, 128 * t) if t < PT else (KTs, PAST)
                for b in range(2):
                    ins = dve.tensor_copy(kt[:, 4 * b:4 * b + 4, at:at + r], P[:, 4 + b, :].rearrange("p (c n) -> p c n", c=4)[:, :, 0:r])
                ins.then_inc(sem("bkT_copied"), 1)

            def q_norm_B(t):
                head_norm(ROWS[t], 0, qn_r, rows_r[:, 0:BD], "q_squared", "q_squares_summed", "q_rms", unit(1, t)).then_inc(sem("q_normed"), 1)

            normalise("mix1", 0)
            q_norm_B(0)
            dve.wait_ge(sem("bk_stored"), 16 * TILES)
            for t in range(TILES):
                attention(1, t)
                if t + 1 < TILES:
                    q_norm_B(t + 1)
                add_mixed(1, t)
            mixer(1)

        @block.gpsimd
        def _(pool):
            for layer in range(2):
                for t in range(TILES):
                    r, u = 128, unit(layer, t)
                    table = a[f"uv{layer}"]
                    for seg, start, steps in segments_of(t):
                        base = first_step(layer, t) + start
                        if start in (0, second_start(t)):
                            pool.wait_ge(sem("experts_chosen"), 2 * u + 1 + (start > 0))
                        with pool.Fori(0, steps) as i:
                            for q in range(GROUPS):
                                nth = i * GROUPS + (GROUPS * base + q + 1)
                                wait_alone(pool, "slots_free", nth, "pool_passed")
                                cols = slice(GROUP * q, GROUP * (q + 1))
                                pool.tensor_copy(stage[0:r, cols], expert[u % 2][0:r, bass.ds(i * SLOTS + (start * SLOTS + GROUP * q), GROUP)])\
                                    .then_inc(sem("indices_staged"), 1)
                                wait_alone(pool, "indices_staged", nth, "pool_passed")
                                for b in range(GROUP * q, GROUP * (q + 1)):
                                    pool.indirect_dma_start(slot[b][0:r, :], None, table,
                                                            bass.IndirectOffsetOnAxis(ap=stage[0:r, b:b + 1], axis=0)).then_inc(sem(f"rows{b}_gathered"), 16)


def program(nc, ins, outs):
    ins = {k: nc.dram_tensor(f"in_{k}", v, F32, kind="ExternalInput").ap() for k, v in ins.items()}
    outs = {k: nc.dram_tensor(f"out_{k}", v, F32, kind="ExternalOutput").ap() for k, v in outs.items()}
    build(nc, ins, outs)


def kernel(x_prompt, x_sample, c_prompt, c_sample, cache_a_ckv, cache_a_krope, cache_b_k, cache_b_v,
           ada_w, ada_b, norm_mix_w, norm_ffn_w, a_w_in, a_q_lora_norm, a_kv_lora_norm, a_w_uq, a_w_ukv,
           a_q_norm, a_k_norm, a_w_o, kv_ada_w, kv_ada_b, kv_norm_w, b_w_kv, b_k_norm, b_w_q, b_q_norm,
           b_rel_bias, b_w_o, p_w_q, p_subkeys, p_u, p_v):
    import concourse.bacc as bacc
    from concourse.bass_utils import run_bass_kernel_spmd

    f = lambda x: np.ascontiguousarray(np.asarray(x))
    pos = np.arange(SEQ, dtype=np.float32)
    freqs = (np.float32(10000.0) ** (-np.arange(HALF, dtype=np.float32) / HALF)).astype(np.float32)
    ang = pos[:, None] * freqs[None, :]
    rope = np.concatenate([np.cos(ang), np.sin(ang)], axis=1).astype(np.float32)
    rope = rope.reshape(PT, 128, ROPE).transpose(1, 0, 2).reshape(128, PT * ROPE)
    masks = np.zeros((128, 128 + CHUNK), np.float32)
    masks[0, 0:CHUNK] = 1.0
    masks[0, 128:] = NEG
    ada = np.concatenate([f(ada_w)[0], f(ada_w)[1], f(kv_ada_w)], axis=1)
    ada = ada.reshape(128, C, ADA_BLOCKS, ADA_BLOCK).transpose(2, 0, 1, 3).reshape(ADA_BLOCKS, 128, C * ADA_BLOCK)
    ukv = f(a_w_ukv)[0].reshape(KV_LORA, HEADS, 2, 64).transpose(0, 2, 1, 3).reshape(KV_LORA, 2 * D)
    rel = f(b_rel_bias)[0]
    ext = np.concatenate([np.repeat(rel[:, 256:257], 384, axis=1), rel[:, 255:0:-1], rel[:, 0:1]], axis=1)
    strips = np.stack([ext[:, 127 - q:127 - q + STRIP] for q in range(128)], axis=1)
    strips[:, 0:CHUNK, STRIP - CHUNK:] = NEG
    arrays = {
        "xp": f(x_prompt)[0], "xs": f(x_sample)[0], "c": np.concatenate([f(c_prompt), f(c_sample)], axis=0),
        "ada_w": ada, "ada_b": np.concatenate([f(ada_b)[0], f(ada_b)[1], f(kv_ada_b)]),
        "norms": np.concatenate([f(norm_mix_w), f(norm_ffn_w), f(kv_norm_w)[None]], axis=0),
        "lora": np.concatenate([f(a_q_lora_norm)[0], f(a_kv_lora_norm)[0]]),
        "qkw": np.concatenate([f(a_q_norm)[0], f(a_k_norm)[0]]),
        "bqk": np.concatenate([f(b_q_norm)[0], f(b_k_norm)]),
        "w_in": f(a_w_in)[0], "w_uq": f(a_w_uq)[0], "w_ukv": ukv, "w_oA": f(a_w_o)[0],
        "past_ckvT": f(cache_a_ckv)[0, 0].T, "past_kr": f(cache_a_krope)[0, 0],
        "past_k": f(cache_b_k)[0].reshape(PAST, D), "past_v": f(cache_b_v)[0].reshape(PAST, D),
        "past_kT": f(cache_b_k)[0].reshape(PAST, D).T,
        "w_kv": f(b_w_kv), "w_q": f(b_w_q)[0], "w_oB": f(b_w_o)[0], "p_w_q": f(p_w_q),
        "bias_strips": strips,
        "skT": f(p_subkeys).transpose(0, 2, 4, 1, 3).reshape(2, 128, PH, NKEYS),
        "uv0": np.concatenate([f(p_u)[0], f(p_v)[0]], axis=1), "uv1": np.concatenate([f(p_u)[1], f(p_v)[1]], axis=1),
        "ident": np.eye(128, dtype=np.float32), "iota": np.tile(np.arange(TOPK, dtype=np.float32), (128, 1)),
        "rope": rope, "masks": masks,
    }
    arrays = {k: np.ascontiguousarray(v) for k, v in arrays.items()}
    shapes = {"y_p": (SEQ, D), "y_s": (DEC, D), "ckv_p": (SEQ, KV_LORA), "kr_p": (SEQ, ROPE), "bk_p": (SEQ, D), "bv_p": (SEQ, D),
              "ckv_s": (DEC, KV_LORA), "kr_s": (DEC, ROPE), "bk_s": (PAST, D), "bv_s": (PAST, D)}
    nc = bacc.Bacc("TRN2", target_bir_lowering=False, num_devices=1)
    program(nc, {k: v.shape for k, v in arrays.items()}, shapes)
    res = run_bass_kernel_spmd(nc, [{f"in_{k}": v for k, v in arrays.items()}], core_ids=[0]).results[0]
    g = {k: res[f"out_{k}"] for k in shapes}
    return (g["y_p"][None], g["y_s"][None], g["ckv_p"][None, None], g["kr_p"][None, None],
            g["bk_p"].reshape(1, SEQ, HEADS, BD), g["bv_p"].reshape(1, SEQ, HEADS, BD),
            g["ckv_s"][None, None], g["kr_s"][None, None],
            g["bk_s"].reshape(1, PAST, HEADS, BD), g["bv_s"].reshape(1, PAST, HEADS, BD))
```
